# Optimizing a Trainium2 kernel written in Bass

```python
import math
import jax, jax.numpy as jnp
from jax import lax
import numpy as np

D_MODEL = 1024
BATCH = 1
SEQ = 1024
DEPTH = 1

CTX_LEN = 256
GRID_W = 64
D_MIX = D_MODEL
D_LRU = D_MIX // 2
LRU_BLOCKS = 8
LRU_BLOCK_W = D_LRU // LRU_BLOCKS
CONV_W = 4
LRU_C = 8.0
GLA_HEADS = 4
D_GLA_V = D_MIX - D_LRU
D_GLA_K = D_GLA_V // 2
GLA_DK = D_GLA_K // GLA_HEADS
GLA_DV = D_GLA_V // GLA_HEADS
GATE_RANK = 16
GATE_TAU = 16.0
GLA_CHUNK = 64
N_EXPERTS = 32
TOP_K = 4
D_EXPERT = D_MODEL
SWIGLU_LIMIT = 7.0
SWIGLU_ALPHA = 1.702
MOE_BLOCK = 128
N_MOD = 6
DEEPNORM_ALPHA = (2.0 * DEPTH) ** 0.25
DEEPNORM_BETA = (8.0 * DEPTH) ** -0.25
LN_EPS = 1e-5
RMS_EPS = 1e-6
SPLIT_SIZES = (D_LRU, D_LRU, D_GLA_K, D_GLA_K, D_GLA_V, D_GLA_V, GATE_RANK)
D_IN = sum(SPLIT_SIZES)
SPLIT_POINTS = tuple(sum(SPLIT_SIZES[:i + 1]) for i in range(len(SPLIT_SIZES) - 1))

kernel_name = "hymba_rglru_gla_moe_dit_layer"

f32 = jnp.float32

def layer_norm(x, g, b):
    xf = x.astype(f32)
    mu = xf.mean(-1, keepdims=True)
    var = jnp.square(xf - mu).mean(-1, keepdims=True)
    return ((xf - mu) * lax.rsqrt(var + LN_EPS) * g.astype(f32) + b.astype(f32)).astype(x.dtype)

def ada_mod(cvec, w, b):
    m = jax.nn.silu(cvec) @ w + b
    return jnp.split(m[..., None, :], N_MOD, axis=-1)

def modulate(x, shift, scale):
    return x * (1.0 + scale) + shift

def centred_dwconv(u, w, b):
    pad_l = CONV_W // 2
    pad_r = CONV_W - 1 - pad_l
    L = u.shape[-2]
    up = jnp.pad(u, [(0, 0)] * (u.ndim - 2) + [(pad_l, pad_r), (0, 0)])
    out = b
    for tap in range(CONV_W):
        out = out + up[..., tap:tap + L, :] * w[tap]
    return out

def to_col_major(t, rows):
    B_, L, C = t.shape
    return t.reshape(B_, rows, GRID_W, C).transpose(0, 2, 1, 3).reshape(B_, L, C)

def from_col_major(t, rows):
    B_, L, C = t.shape
    return t.reshape(B_, GRID_W, rows, C).transpose(0, 2, 1, 3).reshape(B_, L, C)

def _linear_combine(left, right):
    a_l, b_l = left
    a_r, b_r = right
    return a_l * a_r, a_r * b_l + b_r

def rglru_scan(u, h0, w_a, b_a, w_x, b_x, lam):
    B_, L, _ = u.shape
    ub = u.reshape(B_, L, LRU_BLOCKS, LRU_BLOCK_W)
    r = jax.nn.sigmoid(jnp.einsum('blnc,ncd->blnd', ub, w_a).reshape(B_, L, D_LRU) + b_a)
    i = jax.nn.sigmoid(jnp.einsum('blnc,ncd->blnd', ub, w_x).reshape(B_, L, D_LRU) + b_x)
    log_a = (-LRU_C * jax.nn.softplus(-lam.astype(f32))) * r.astype(f32)
    a = jnp.exp(log_a)
    b = jnp.sqrt(-jnp.expm1(2.0 * log_a)) * (i * u).astype(f32)
    b = b.at[:, 0].add(a[:, 0] * h0)
    _, h = lax.associative_scan(_linear_combine, (a, b), axis=1)
    return h

def gla_chunked(q, k, v, log_alpha, s0):
    B_, H, L, _ = q.shape
    n = L // GLA_CHUNK

    def chunks(t):
        return t.astype(f32).reshape(B_, H, n, GLA_CHUNK, t.shape[-1])

    qc, kc, vc, lac = chunks(q), chunks(k), chunks(v), chunks(log_alpha)
    bcum = jnp.cumsum(lac, axis=-2)
    btot = bcum[..., -1:, :]
    q_dec = qc * jnp.exp(bcum)
    k_dec = kc * jnp.exp(-bcum)
    k_end = kc * jnp.exp(btot - bcum)
    mask = jnp.tril(jnp.ones((GLA_CHUNK, GLA_CHUNK), dtype=bool))
    scores = jnp.where(mask, jnp.einsum('bhnik,bhnjk->bhnij', q_dec, k_dec), 0.0)
    o_intra = jnp.einsum('bhnij,bhnjv->bhniv', scores, vc)
    chunk_kv = jnp.einsum('bhnjk,bhnjv->bhnkv', k_end, vc)
    decay_tot = jnp.exp(btot[..., 0, :])

    def step(s, inp):
        dec, kv = inp
        return dec[..., None] * s + kv, s

    s_final, s_starts = lax.scan(step, s0, (jnp.moveaxis(decay_tot, 2, 0), jnp.moveaxis(chunk_kv, 2, 0)))
    s_starts = jnp.moveaxis(s_starts, 0, 2)
    o_inter = jnp.einsum('bhnik,bhnkv->bhniv', q_dec, s_starts)
    o = (o_intra + o_inter).reshape(B_, H, L, GLA_DV)
    return o, s_final

def mix_stream(u, rows, lru_init, gla_init, w_in, conv_w, conv_b, lru_wa, lru_ba, lru_wx, lru_bx,
               lru_lam, gla_wa, gla_ba):
    B_, L, _ = u.shape
    proj = u @ w_in
    x_lru, gate_lru, q, k, v, g, a_low = jnp.split(proj, SPLIT_POINTS, axis=-1)
    if rows is None:
        x_lru = centred_dwconv(x_lru, conv_w, conv_b)
    else:
        x_lru = centred_dwconv(x_lru.reshape(B_, rows, GRID_W, D_LRU), conv_w, conv_b).reshape(B_, L, D_LRU)
        q, k, v, a_low = (to_col_major(t, rows) for t in (q, k, v, a_low))

    def heads(t):
        return t.reshape(B_, L, GLA_HEADS, -1).transpose(0, 2, 1, 3)

    qh = heads(q) * (GLA_DK ** -0.5)
    kh = heads(k)
    vh = heads(v)
    lru_states, gla_states, h_dirs, o_dirs = [], [], [], []
    for d in range(2):
        xs = x_lru if d == 0 else jnp.flip(x_lru, 1)
        h = rglru_scan(xs, lru_init[d], lru_wa[d], lru_ba[d], lru_wx[d], lru_bx[d], lru_lam[d])
        lru_states.append(h[:, -1])
        h_dirs.append(h if d == 0 else jnp.flip(h, 1))
        la = heads(jax.nn.log_sigmoid((a_low @ gla_wa[d] + gla_ba[d]).astype(f32)) / GATE_TAU)
        seqs = (qh, kh, vh, la) if d == 0 else tuple(jnp.flip(t, 2) for t in (qh, kh, vh, la))
        o, s = gla_chunked(*seqs, gla_init[d])
        gla_states.append(s)
        o_dirs.append(o if d == 0 else jnp.flip(o, 2))
    h_lru = h_dirs[0] + h_dirs[1]
    o_gla = (o_dirs[0] + o_dirs[1]).transpose(0, 2, 1, 3).reshape(B_, L, D_GLA_V)
    if rows is not None:
        o_gla = from_col_major(o_gla, rows)
    return (h_lru, gate_lru, o_gla, g), jnp.stack(lru_states), jnp.stack(gla_states)

def merge_heads(h_lru, gate_lru, o_gla, g, gla_norm_g, w_out):
    y_lru = h_lru * jax.nn.gelu(gate_lru.astype(f32))
    B_, L, _ = o_gla.shape
    oh = o_gla.reshape(B_, L, GLA_HEADS, GLA_DV)
    oh = oh * lax.rsqrt(jnp.mean(jnp.square(oh), -1, keepdims=True) + RMS_EPS)
    y_gla = oh.reshape(B_, L, D_GLA_V) * gla_norm_g.astype(f32) * jax.nn.silu(g.astype(f32))
    y = jnp.concatenate([y_lru, y_gla], axis=-1).astype(w_out.dtype)
    return y @ w_out

def moe_ffn(h, w_router, b_router, w_gate, b_gate, w_up, b_up, w_down, b_down):
    B_, L, D = h.shape
    xt = h.reshape(-1, D)
    T = xt.shape[0]
    logits = (xt @ w_router + b_router).astype(f32)
    top_v, top_i = lax.top_k(logits, TOP_K)
    top_w = jax.nn.softmax(top_v, axis=-1)
    n_assign = T * TOP_K
    expert_flat = top_i.reshape(-1)
    token_flat = jnp.arange(n_assign, dtype=jnp.int32) // TOP_K
    w_flat = top_w.reshape(-1)
    order = jnp.argsort(expert_flat)
    e_sorted = expert_flat[order]
    counts = jnp.bincount(expert_flat, length=N_EXPERTS)
    starts = jnp.cumsum(counts) - counts
    padded = (counts + MOE_BLOCK - 1) // MOE_BLOCK * MOE_BLOCK
    pad_ends = jnp.cumsum(padded)
    pad_starts = pad_ends - padded
    rank = jnp.arange(n_assign, dtype=jnp.int32) - starts[e_sorted]
    dest = pad_starts[e_sorted] + rank
    n_blocks = -(-(n_assign + N_EXPERTS * (MOE_BLOCK - 1)) // MOE_BLOCK)
    n_rows = n_blocks * MOE_BLOCK
    row_token = jnp.zeros((n_rows,), jnp.int32).at[dest].set(token_flat[order])
    row_weight = jnp.zeros((n_rows,), f32).at[dest].set(w_flat[order])
    block_expert = jnp.minimum(
        jnp.searchsorted(pad_ends, jnp.arange(n_blocks, dtype=jnp.int32) * MOE_BLOCK, side='right'),
        N_EXPERTS - 1)

    def expert_block(args):
        tok, e = args
        xb = xt[tok]
        gate = jnp.minimum(xb @ w_gate[e] + b_gate[e], SWIGLU_LIMIT)
        up = jnp.clip(xb @ w_up[e] + b_up[e], -SWIGLU_LIMIT, SWIGLU_LIMIT)
        act = (up + 1.0) * gate * jax.nn.sigmoid(SWIGLU_ALPHA * gate)
        return act @ w_down[e] + b_down[e]

    y_rows = lax.map(expert_block, (row_token.reshape(n_blocks, MOE_BLOCK), block_expert))
    y_rows = y_rows.reshape(n_rows, D) * row_weight[:, None].astype(y_rows.dtype)
    y = jnp.zeros_like(xt).at[row_token].add(y_rows.astype(xt.dtype))
    return y.reshape(B_, L, D)

def setup_inputs(seed: int = 0) -> dict:
    key = jax.random.key(seed)
    ks = jax.random.split(key, 32)
    nrm = lambda k, shape, s: jax.random.normal(k, shape, f32) * s
    a_init = jax.random.uniform(ks[13], (DEPTH, 2, D_LRU), f32, 0.9, 0.999)
    root = a_init ** (1.0 / LRU_C)
    lru_lam = jnp.log(root) - jnp.log1p(-root)
    return {
        "x": nrm(ks[0], (BATCH, SEQ, D_MODEL), 1.0),
        "c": nrm(ks[1], (BATCH, D_MODEL), 1.0),
        "ctx": nrm(ks[2], (BATCH, CTX_LEN, D_MODEL), 1.0),
        "c_ctx": nrm(ks[3], (D_MODEL,), 1.0),
        "w_ada": nrm(ks[4], (DEPTH, D_MODEL, N_MOD * D_MODEL), 0.5 * D_MODEL ** -0.5),
        "b_ada": nrm(ks[5], (DEPTH, N_MOD * D_MODEL), 0.02),
        "w_in": nrm(ks[6], (DEPTH, D_MODEL, D_IN), D_MODEL ** -0.5),
        "conv_w": nrm(ks[7], (DEPTH, CONV_W, D_LRU), CONV_W ** -0.5),
        "conv_b": nrm(ks[8], (DEPTH, D_LRU), 0.02),
        "lru_wa": nrm(ks[9], (DEPTH, 2, LRU_BLOCKS, LRU_BLOCK_W, LRU_BLOCK_W), LRU_BLOCK_W ** -0.5),
        "lru_ba": nrm(ks[10], (DEPTH, 2, D_LRU), 0.02),
        "lru_wx": nrm(ks[11], (DEPTH, 2, LRU_BLOCKS, LRU_BLOCK_W, LRU_BLOCK_W), LRU_BLOCK_W ** -0.5),
        "lru_bx": nrm(ks[12], (DEPTH, 2, D_LRU), 0.02),
        "lru_lam": lru_lam,
        "gla_wa": nrm(ks[14], (DEPTH, 2, GATE_RANK, D_GLA_K), GATE_RANK ** -0.5),
        "gla_ba": nrm(ks[15], (DEPTH, 2, D_GLA_K), 0.1),
        "gla_norm_g": 1.0 + nrm(ks[16], (DEPTH, D_GLA_V), 0.02),
        "w_out": nrm(ks[17], (DEPTH, D_MIX, D_MODEL), DEEPNORM_BETA * D_MIX ** -0.5),
        "ln1_g": 1.0 + nrm(ks[18], (DEPTH, D_MODEL), 0.02),
        "ln1_b": nrm(ks[19], (DEPTH, D_MODEL), 0.02),
        "w_router": nrm(ks[20], (DEPTH, D_MODEL, N_EXPERTS), D_MODEL ** -0.5),
        "b_router": nrm(ks[21], (DEPTH, N_EXPERTS), 0.01),
        "w_gate": nrm(ks[22], (DEPTH, N_EXPERTS, D_MODEL, D_EXPERT), D_MODEL ** -0.5),
        "b_gate": nrm(ks[23], (DEPTH, N_EXPERTS, D_EXPERT), 0.02),
        "w_up": nrm(ks[24], (DEPTH, N_EXPERTS, D_MODEL, D_EXPERT), D_MODEL ** -0.5),
        "b_up": nrm(ks[25], (DEPTH, N_EXPERTS, D_EXPERT), 0.02),
        "w_down": nrm(ks[26], (DEPTH, N_EXPERTS, D_EXPERT, D_MODEL), DEEPNORM_BETA * D_EXPERT ** -0.5),
        "b_down": nrm(ks[27], (DEPTH, N_EXPERTS, D_MODEL), 0.02),
        "ln2_g": 1.0 + nrm(ks[28], (DEPTH, D_MODEL), 0.02),
        "ln2_b": nrm(ks[29], (DEPTH, D_MODEL), 0.02),
    }

def reference(x, c, ctx, c_ctx, w_ada, b_ada, w_in, conv_w, conv_b, lru_wa, lru_ba, lru_wx, lru_bx,
              lru_lam, gla_wa, gla_ba, gla_norm_g, w_out, ln1_g, ln1_b, w_router, b_router, w_gate,
              b_gate, w_up, b_up, w_down, b_down, ln2_g, ln2_b):
    B_ = x.shape[0]
    rows = x.shape[1] // GRID_W
    zero_lru = jnp.zeros((2, B_, D_LRU), f32)
    zero_gla = jnp.zeros((2, B_, GLA_HEADS, GLA_DK, GLA_DV), f32)
    for l in range(DEPTH):
        sh1, sc1, g1, sh2, sc2, g2 = ada_mod(c, w_ada[l], b_ada[l])
        sh1c, sc1c, g1c, sh2c, sc2c, g2c = ada_mod(c_ctx[None], w_ada[l], b_ada[l])
        mix_params = (w_in[l], conv_w[l], conv_b[l], lru_wa[l], lru_ba[l], lru_wx[l], lru_bx[l],
                      lru_lam[l], gla_wa[l], gla_ba[l])
        raw_ctx, lru_ctx_state, gla_ctx_state = mix_stream(
            modulate(ctx, sh1c, sc1c), None, zero_lru, zero_gla, *mix_params)
        raw_lat, _, _ = mix_stream(
            modulate(x, sh1, sc1), rows, lru_ctx_state, gla_ctx_state, *mix_params)
        y = merge_heads(*raw_lat, gla_norm_g[l], w_out[l])
        x = layer_norm(DEEPNORM_ALPHA * x + g1 * y, ln1_g[l], ln1_b[l])
        moe_params = (w_router[l], b_router[l], w_gate[l], b_gate[l], w_up[l], b_up[l], w_down[l], b_down[l])
        x = layer_norm(DEEPNORM_ALPHA * x + g2 * moe_ffn(modulate(x, sh2, sc2), *moe_params),
                       ln2_g[l], ln2_b[l])
        if l < DEPTH - 1:
            y_c = merge_heads(*raw_ctx, gla_norm_g[l], w_out[l])
            ctx = layer_norm(DEEPNORM_ALPHA * ctx + g1c * y_c, ln1_g[l], ln1_b[l])
            ctx = layer_norm(DEEPNORM_ALPHA * ctx + g2c * moe_ffn(modulate(ctx, sh2c, sc2c), *moe_params),
                             ln2_g[l], ln2_b[l])
    return x


_drawn_inputs = setup_inputs


def setup_inputs(seed=0):
    import zlib

    import numpy as np

    out = dict(_drawn_inputs(seed))
    spreads = {}
    factors = {'ctx': 4.037,
     'conv_b': 3.101,
     'lru_ba': 64.0,
     'lru_bx': 119.883,
     'gla_wa': 4.223,
     'gla_ba': 8.0,
     'gla_norm_g': 37.414,
     'b_router': 32.773,
     'b_gate': 31.714,
     'b_up': 43.958,
     'b_down': 8.0,
     'ln2_g': 7.34,
     'ln2_b': 21.507}
    for name, (base, spread) in spreads.items():
        noise = np.random.default_rng([zlib.crc32(name.encode()), seed]).standard_normal(out[name].shape)
        drawn = base * np.exp(spread * noise) if base else spread * noise
        out[name] = __import__('jax').numpy.asarray(drawn.astype(out[name].dtype))
    for name, factor in factors.items():
        out[name] = (out[name] * factor).astype(out[name].dtype)
    return out
```

```python
from contextlib import ExitStack

import concourse.bass as bass
from concourse import mybir

ALU = mybir.AluOpType
ACT = mybir.ActivationFunctionType
AX_X = mybir.AxisListType.X
F32 = mybir.dt.float32
I32 = mybir.dt.int32
U32 = mybir.dt.uint32

P = 128
BANK = 512
ds = bass.ds


class Chain:

    def __init__(self, eng, sem):
        self.eng, self.sem, self.n = eng, sem, 0

    def link(self, ins):
        self.n += 1
        ins.then_inc(self.sem, 1)
        self.eng.wait_ge(self.sem, self.n)


def layer(nc, x, c, ctx, c_ctx, w_ada, b_ada, w_in, conv_w, conv_b, lru_wa, lru_ba, lru_wx, lru_bx,
          lru_lam, gla_wa, gla_ba, gla_norm_g, w_out, ln1_g, ln1_b, w_router, b_router, w_gate,
          b_gate, w_up, b_up, w_down, b_down, ln2_g, ln2_b, out):
    SEQ, D = x.shape[1], x.shape[2]
    CTX = ctx.shape[1]
    L = SEQ + CTX
    GRID_W = 64
    ROWS = SEQ // GRID_W
    KD = D // P
    NT, NTC = SEQ // P, CTX // P
    D_LRU = conv_w.shape[2]
    JL = D_LRU // P
    DK, DV = 64, 128
    HEADS = (D - D_LRU) // DV
    PAIRS = HEADS // 2
    RANK = gla_wa.shape[2]
    CH = 64
    NCH, NCHC = SEQ // CH, CTX // CH
    NE, TOPK = w_router.shape[2], 4
    ALPHA = 2.0 ** 0.25
    LN_EPS, RMS_EPS = 1e-5, 1e-6
    LIMIT, SWIGLU = 7.0, 1.702
    WU = 256
    STEP = 32
    NCLS = WU // STEP
    CLASSES = range(P // STEP, NCLS + 1)
    MAXU = NE - 1 + SEQ * TOPK // WU
    PIECES = 12
    MAXROWS = SEQ * TOPK + NE * P
    BLOCKS = MAXROWS // P + 1
    NOSLOT = 1 << 20
    segs_all = [(0, 512), (512, 1024), (1024, L)]
    segs_lat = segs_all[:2]

    h2_dram = nc.dram_tensor("h2_rows", [SEQ, D], F32).ap()
    y_dram = nc.dram_tensor("expert_rows", [TOPK * SEQ, D], F32).ap()
    rowslot_dram = nc.dram_tensor("row_slot", [MAXROWS + P, 1], I32).ap()
    tab_dram = nc.dram_tensor("unit_table", [P, 4], I32).ap()

    ctxs = ExitStack()
    with ctxs:
        def sb(name, shape, dt=F32):
            return ctxs.enter_context(nc.sbuf_tensor(name, shape, dt))

        def sem(name):
            return ctxs.enter_context(nc.semaphore(name))

        ident = sb("ident", [P, P])
        ones = sb("ones", [P, P])
        tri = sb("tri", [P, P])
        masks = sb("masks", [P, 2, P], I32)
        par = sb("par", [P, 84])
        ada1 = sb("ada1", [P, 2, KD, 2])
        adarow = sb("adarow", [P, 4, D])
        lruw = sb("lruw", [P, 16, P])
        cl = sb("cl", [P, 2 * JL])
        ncl = sb("ncl", [P, 2 * JL])
        small = sb("small", [P, 64])
        tab = sb("tab", [1, 4 * P], I32)
        C_C, C_CTX, C_BADA, C_CONVW, C_CONVB = 0, 8, 16, 32, 48
        C_BA, C_BX, C_LAM, C_GBA, C_GN, NPAR = 52, 60, 68, 76, 80, 84

        AW = 45056
        arena = sb("arena", [P, AW])

        def reg(off, *shape):
            n = 1
            for s in shape:
                n *= s
            assert off + n <= AW
            v = arena[:, off:off + n]
            if len(shape) == 2:
                v = v.rearrange("p (a b) -> p a b", a=shape[0])
            if len(shape) == 3:
                v = v.rearrange("p (a b c) -> p a b c", a=shape[0], b=shape[1])
            if len(shape) == 4:
                v = v.rearrange("p (a b c d) -> p a b c d", a=shape[0], b=shape[1], c=shape[2])
            return v

        O_YT, O_XL, O_QT, O_KT, O_V, O_AL, O_R = 0, 8192, 13312, 15360, 17920, 23040, 24320
        YT = reg(O_YT, KD, SEQ)
        XL = reg(O_XL, JL, L)
        QT = reg(O_QT, PAIRS, SEQ)
        KT = reg(O_KT, PAIRS, L)
        V = reg(O_V, NT + NTC, HEADS * DV)
        AL = reg(O_AL, L)
        wada_ring = reg(0, 3, KD, 512)
        csb = reg(12288, KD, P)
        prow = reg(O_R, P)
        xin = reg(O_QT, NT + NTC, D)
        uT = reg(O_R, KD, L)
        wv = reg(O_R + 10240, KD, 512)
        WRING = 6
        wring = [reg(O_R + 14336 + 1024 * s, KD, P) for s in range(WRING)]
        lA = reg(O_R, JL, L)
        lB = reg(O_R + 5120, JL, L)
        lC = reg(O_R + 10240, JL, L)
        lH = reg(O_R + 15360, JL, SEQ)
        lT = reg(O_R + 19456, L)
        O_G = O_XL
        gBC = reg(O_XL, 2, L)
        gE = reg(O_XL + 2560, L)
        gMask = [reg(O_XL + 3840, L), reg(O_R, L)]
        o = O_R + 1280
        gQ = reg(o, 2, SEQ); o += 2048
        gK = reg(o, 2, SEQ); o += 2048
        gKE = reg(o, 2, L); o += 2560
        gKT = reg(o, 2, NT + NTC, P); o += 2560
        NSLOT = 2 + NCH
        gS = reg(o, 2, NSLOT, 2, DV); o += 2 * NSLOT * 2 * DV
        gSc = reg(o, 2, 2, 2, P); o += 1024
        assert o <= AW
        gO = reg(O_XL, 2, SEQ)
        gSq = reg(O_R + 1280 + 4096, 2, SEQ)
        wout = reg(O_QT, KD, D)
        O_X1 = 24576
        X1 = reg(O_X1, NT, D)
        o = O_X1 + 8192
        xres = reg(o, 2, D); o += 2048
        ybuf = reg(o, 2, D); o += 2048
        h2b = reg(o, 2, D); o += 2048
        h2T = reg(o, KD, P); o += 1024
        ln1r = reg(o, 2, D); o += 2048
        wrt = reg(o, KD, NE); o += 256
        brow = reg(o, 2, D); o += 2048
        O_RT = o
        lgt = reg(O_RT, NT, NE)
        assert O_RT + 256 <= AW
        o = O_X1 + 8192 + 2048
        OH = reg(o, TOPK, NT, NE); o += 1024
        tmpO = reg(o, NT, NE); o += 256
        Mx = reg(o, NT, NE); o += 256
        Gx = reg(o, NT, NE); o += 256
        Wd = reg(o, NT, NE); o += 256
        mx8 = reg(o, NT, 8); o += 64
        ix8 = reg(o, NT, 8).bitcast(U32); o += 64
        ixf = reg(o, NT, 8); o += 64
        ev = reg(o, NT, TOPK); o += 32
        iot = reg(o, NE); o += 32
        rt = reg(o, 16, NE); o += 512
        assert o <= O_X1 + 8192 + 6144
        WdT = reg(O_RT - 2048 - 256 - 2048 - 1024, P)
        lw = lruw[:, :, :].rearrange("p a b -> p (a b)")
        bgT = lw[:, 0:256].rearrange("p (k e) -> p k e", k=KD)
        buT = lw[:, 256:512].rearrange("p (k e) -> p k e", k=KD)
        topw = lw[:, 512:544].rearrange("p (t k) -> p t k", t=NT)
        dest = lw[:, 544:576].bitcast(U32).rearrange("p (k t) -> p k t", k=TOPK)
        slotid = lw[:, 800:832].bitcast(I32).rearrange("p (k t) -> p k t", k=TOPK)
        bgc = lw[:, 592:600]
        buc = lw[:, 600:608]
        gidx = lw[:, 608:610].bitcast(U32)
        sidx = lw[:, 612:614].bitcast(U32)
        brt = lw[:, 640:672]
        ioti2 = lw[:, 672:704].bitcast(I32)
        wa_sb = lw[0:RANK, 1024:1536].rearrange("p (a b) -> p a b", a=2)
        tabc = small[:, 40:44].bitcast(I32)
        fmask = reg(AW - P, P)
        eps_ln, eps_rms = sb("eps_ln", [P, 1]), sb("eps_rms", [P, 1])
        csil = sb("csil", [P, KD, 2])
        rowslot = lw[:, 704:704 + BLOCKS].bitcast(I32)
        rowtok = lw[:, 896:896 + BLOCKS].bitcast(I32)
        bdn = reg(O_X1 + 8192 + 6144 + 1024, 1, D)
        ring = [reg(2048 * q, 2, D) for q in range(PIECES)]
        o = O_X1 + 8192
        xg = reg(o, 2, D); o += 2048
        xT = reg(o, KD, WU); o += 2048
        gb = reg(o, KD, WU); o += 2048
        sg = reg(o, KD, WU); o += 2048
        act_ = reg(o, KD, WU); o += 2048
        yb = reg(o, 2, D); o += 2048
        assert o <= AW
        yrows = [reg(TOPK * 1024 * b, TOPK, D) for b in range(2)]
        acc = reg(8192, 2, D)
        ln2r = reg(10240, 2, D)
        fin = reg(12288, 2, D)

        ps = [ctxs.enter_context(nc.psum_tensor(f"ps{i}", [P, BANK], F32)) for i in range(8)]

        settled = {e.engine: sem(f"settled{i}") for i, e in enumerate((nc.scalar, nc.vector, nc.gpsimd))}
        var_ready, std_ready = sem("var_ready"), sem("std_ready")
        vch, ach, pch = sem("vector_chain"), sem("scalar_chain"), sem("pool_chain")
        const_ready = sem("const_ready")
        d_par, d_lruw, d_bada, d_wv, d_small = sem("d_par"), sem("d_lruw"), sem("d_bada"), sem("d_wv"), sem("d_small")
        d_wada = [sem(f"d_wada{i}") for i in range(3)]
        d_x = [sem(f"d_x{i}") for i in range(3)]
        d_win = [sem(f"d_win{i}") for i in range(WRING)]
        par_turned, par_ready, cs_ready, csb_ready = sem("par_turned"), sem("par_ready"), sem("cs_ready"), sem("csb_ready")
        ada_used, ada1_ready, adarow_done = sem("ada_used"), sem("ada1_ready"), sem("adarow_done")
        x_turned, uT_act, uT_dve = sem("x_turned"), sem("uT_act"), sem("uT_dve")
        proj_done, proj_act, proj_dve, conv_started = sem("proj_done"), sem("proj_act"), sem("proj_dve"), sem("conv_started")
        lru_mm, lru_sig, lru_exp, lru_b2, lru_sqrt, lru_ix, lru_done, cl_ready = (
            sem("lru_mm"), sem("lru_sig"), sem("lru_exp"), sem("lru_b2"), sem("lru_sqrt"), sem("lru_ix"),
            sem("lru_done"), sem("cl_ready"))
        z_mm, z_min, z_abs, z_ln, cum_done, eq_act, eq_dve, q_done = (
            sem("z_mm"), sem("z_min"), sem("z_abs"), sem("z_ln"), sem("cum_done"), sem("eq_act"),
            sem("eq_dve"), sem("q_done"))
        ke_turned, ke_ready, kv_mm, s_ready, s_zero, gmask_ready = (
            sem("ke_turned"), sem("ke_ready"), sem("kv_mm"), sem("s_ready"), sem("s_zero"), sem("gmask_ready"))
        sc_mm, sc_ready, o_mm, o_ready, sq_ready, rms_mm, rms_act, gla_done = (
            sem("sc_mm"), sem("sc_ready"), sem("o_mm"), sem("o_ready"), sem("sq_ready"), sem("rms_mm"),
            sem("rms_act"), sem("gla_done"))
        d_wout, d_ln1 = sem("d_wout"), sem("d_ln1")
        d_xres = [sem("d_xres0"), sem("d_xres1")]
        out_mm, y_gated, x1_ready, h2_ready, h2_stored, h2_turned, h2T_ready, logit_mm = (
            sem("out_mm"), sem("y_gated"), sem("x1_ready"), sem("h2_ready"), [sem("h2_stored0"), sem("h2_stored1")],
            sem("h2_turned"), sem("h2T_ready"), sem("logit_mm"))
        d_rt, bias_turned, bias_ready, sel_ready, rank_mm, dest_ready, wd_ready, wd_turned, wdT_ready, bd_mm, bd_used = (
            sem("d_rt"), sem("bias_turned"), sem("bias_ready"), sem("sel_ready"), sem("rank_mm"),
            sem("dest_ready"), sem("wd_ready"), sem("wd_turned"), sem("wdT_ready"), sem("bd_mm"), sem("bd_used"))
        iota_ready, top_exp_in, top_exp, tab_stored, tab_ready, rt_zeroed, rt_scattered = (
            sem("iota_ready"), sem("top_exp_in"), sem("top_exp"), sem("tab_stored"), sem("tab_ready"),
            sem("rt_zeroed"), sem("rt_scattered"))
        d_rowslot = sem("d_rowslot")
        tab_col, d_bdn, moe_clear = sem("tab_col"), sem("d_bdn"), sem("moe_clear")
        d_w = [sem(f"d_w{q}") for q in range(PIECES)]
        w_used, d_idx, xg_ready = sem("w_used"), sem("d_idx"), sem("xg_ready")
        mx_turned, xT_act, xT_dve = sem("mx_turned"), sem("xT_act"), sem("xT_dve")
        bias_now = sem("bias_now")
        g_ready, sg_ready, gs_ready, t_ready, act_ready = (
            sem("g_ready"), sem("sg_ready"), sem("gs_ready"), sem("t_ready"), sem("act_ready"))
        y_act, y_dve, y_stored = sem("y_act"), sem("y_dve"), sem("y_stored")
        d_yr = [sem("d_yr0"), sem("d_yr1")]
        gidx_ready, sidx_ready = sem("gidx_ready"), sem("sidx_ready")
        yr_used, d_ln2, fin_ready = sem("yr_used"), sem("d_ln2"), sem("fin_ready")
        fin_stored = [sem("fin_stored0"), sem("fin_stored1")]
        y0_scaled, xn_in, xn_ready = sem("y0_scaled"), sem("xn_in"), sem("xn_ready")

        CQ, CK, CV = 2 * D_LRU, 2 * D_LRU + PAIRS * P, 2 * D_LRU + 2 * PAIRS * P
        CG = CV + HEADS * DV
        CA = CG + HEADS * DV
        jobs = [("v", T, None, None) for T in range(NT + NTC)]
        tiles = [("conv", j, j * P, P) for j in range(JL)]
        tiles += [("k", j, CK + j * P, P) for j in range(PAIRS)]
        tiles += [("alow", 0, CA, RANK)]
        tiles += [("q", j, CQ + j * P, P) for j in range(PAIRS)]
        tiles += [("gate", j, D_LRU + j * P, P) for j in range(JL)]
        tiles += [("g", j, CG + j * P, P) for j in range(HEADS)]
        for n, (kind, j, c0, w) in enumerate(tiles):
            for s in (segs_all if kind in ("conv", "k", "alow") else segs_lat):
                jobs.append((kind, j, s, n))
        by_act = [k in ("gate", "g") or (k == "v" and j % 2 == 0) for k, j, _, _ in jobs]
        counts, freed = [0, 0], []
        for a in by_act:
            counts[0 if a else 1] += 1
            freed.append((0 if a else 1, counts[0 if a else 1]))
        NPA, NPV = counts
        last_tile = {n: i for i, (_, _, _, n) in enumerate(jobs)}
        NCONV = 3 * JL

        def arena_rev(ap, n):
            return ap[:, n - 1::-1]

        def uT_in(n):
            v = ps[4 + n % 4]
            return v[:, :].rearrange("p (r w) -> p r w", w=GRID_W) if n < 16 else v[:, 0:CTX]

        def uT_out(n):
            return colmajor(uT[:, n % 8, 0:SEQ], 8 * (n // 8), 8) if n < 16 else uT[:, n % 8, SEQ:L]

        def grid_half(ap, seg):
            w0, w1 = seg[0] // ROWS, seg[1] // ROWS
            return ap.rearrange("p (r w) -> p w r", w=GRID_W)[:, w0:w1, :]

        def half(ap):
            return ap[:, :].rearrange("p (w r) -> p w r", r=ROWS)

        def colmajor(ap, r0, nr):
            return ap.rearrange("p (w r) -> p r w", r=ROWS)[:, r0:r0 + nr, :]

        order = [[NCH + i for i in range(NCHC)] + list(range(NCH)),
                 [NCH + NCHC - 1 - i for i in range(NCHC)] + list(range(NCH))[::-1]]

        def slot(n):
            return n % 2 if n < NCHC else 2 + n - NCHC

        NS = NCHC + NCH

        def settle(eng):
            eng.sem_inc(settled[eng.engine], 1)

        block = ctxs.enter_context(nc.Block())

        @block.sync
        def _(sp):
            def rows(src, n):
                return src.rearrange("(a b) -> a b", b=P) if n else src

            at = [0]

            def param(ap, n):
                sp.dma_start(prow[at[0]:at[0] + n, :], ap).then_inc(d_par, 16)
                at[0] += n

            param(c[0].rearrange("(a b) -> a b", b=P), 8)
            param(c_ctx.rearrange("(a b) -> a b", b=P), 8)
            param(b_ada[0, 0:2 * D].rearrange("(a b) -> a b", b=P), 16)
            param(conv_w[0].rearrange("t (a b) -> (t a) b", b=P), 16)
            param(conv_b[0].rearrange("(a b) -> a b", b=P), 4)
            for v in (lru_ba, lru_bx, lru_lam):
                param(v[0].rearrange("d (a b) -> (d a) b", b=P), 8)
            param(gla_ba[0].rearrange("d (a b) -> (d a) b", b=P), 4)
            param(gla_norm_g[0].rearrange("(a b) -> a b", b=P), 4)
            wada_v = w_ada[0].rearrange("(k p) n -> p k n", p=P)

            def ada_piece(j):
                if j >= 3:
                    sp.wait_ge(ada_used, j - 2)
                sp.dma_start(wada_ring[:, j % 3], wada_v[:, :, j * 512:(j + 1) * 512]).then_inc(d_wada[j % 3], 16)

            for j in range(4):
                ada_piece(j)
            x_v = x[0].rearrange("(t p) d -> p t d", p=P)
            sp.dma_start(xin[:, 0:4], x_v[:, 0:4]).then_inc(d_x[0], 16)
            sp.dma_start(xin[:, 4:8], x_v[:, 4:8]).then_inc(d_x[1], 16)
            sp.dma_start(xin[:, 8:10], ctx[0].rearrange("(t p) d -> p t d", p=P)).then_inc(d_x[2], 16)
            sp.dma_start(adarow[:, :, :].rearrange("p a b -> p (a b)"),
                         b_ada[0:1, 2 * D:6 * D].partition_broadcast(P).rearrange("p a n -> p (a n)")).then_inc(d_bada, 16)
            for j in range(4, 12):
                ada_piece(j)
            sp.wait_ge(const_ready, 2)
            for d in range(2):
                for g, w in ((0, lru_wa), (1, lru_wx)):
                    for h in range(2):
                        q = (d * 2 + g) * JL
                        sp.dma_start(lruw[64 * h:64 * h + 64, q:q + JL, 64 * h:64 * h + 64],
                                     w[0, d].rearrange("(j h) c e -> h c j e", h=2)[h]).then_inc(d_lruw, 16)
            win_v = w_in[0].rearrange("(k p) n -> p k n", p=P)
            sp.dma_start(wv, win_v[:, :, CV:CV + 512]).then_inc(d_wv, 16)
            for n, (kind, j, c0, w) in enumerate(tiles):
                if n >= WRING:
                    sp.wait_ge(proj_done, last_tile[n - WRING] + 1)
                sp.dma_start(wring[n % WRING][:, :, 0:w], win_v[:, :, c0:c0 + w]).then_inc(d_win[n % WRING], 16)
            sp.wait_ge(lru_done, 2 * JL)
            sp.dma_start(wa_sb, gla_wa[0].rearrange("d r n -> r d n")).then_inc(d_small, 16)
            sp.wait_ge(gla_done, 4)
            sp.dma_start(wout, w_out[0].rearrange("(k p) n -> p k n", p=P)).then_inc(d_wout, 16)
            for i, v in enumerate((ln1_g, ln1_b)):
                sp.dma_start(ln1r[:, i], v.partition_broadcast(P).rearrange("p a n -> p (a n)")).then_inc(d_ln1, 16)
            sp.dma_start(wrt, w_router[0].rearrange("(k p) e -> p k e", p=P)).then_inc(d_rt, 16)
            sp.dma_start(brt, b_router.partition_broadcast(P).rearrange("p a n -> p (a n)")).then_inc(d_rt, 16)
            sp.dma_start(brow[0:NE, 0], b_gate[0]).then_inc(d_rt, 16)
            sp.dma_start(brow[0:NE, 1], b_up[0]).then_inc(d_rt, 16)
            for t in range(NT + 1):
                if t < NT:
                    if t >= 2:
                        sp.wait_ge(x1_ready, t - 1)
                    sp.dma_start(xres[:, t % 2], x[0, t * P:(t + 1) * P, :]).then_inc(d_xres[t % 2], 16)
                if t >= 1:
                    sp.wait_ge(h2_ready, t)
                    sp.dma_start(h2_dram[(t - 1) * P:t * P, :], h2b[:, (t - 1) % 2]).then_inc(h2_stored[(t - 1) % 2], 16)
            sp.wait_ge(x1_ready, NT)
            sp.dma_start(bdn[0:NE], b_down[0].unsqueeze(1)).then_inc(d_bdn, 16)
            sp.wait_ge(tab_col, 1)
            sp.dma_start(tab_dram, tabc).then_inc(tab_stored, 16)
            sp.wait_ge(tab_stored, 16)
            sp.dma_start(tab[0:1, :], tab_dram.rearrange("a b -> (a b)").unsqueeze(0)).then_inc(tab_ready, 16)
            sp.wait_ge(tab_ready, 16)
            def weights(q):
                return (w_gate, w_up, w_down)[q // 4][0].rearrange("e (q c p) n -> e q p c n", c=2, p=P)[:, q % 4]

            def piece(q, e):
                sp.dma_start(ring[q], weights(q)[ds(e, 1)].rearrange("a p c n -> p (a c) n")).then_inc(d_w[q], 16)

            e0 = sp.value_load(tab[0:1, 1:2], min_val=0, max_val=NE - 1)
            for q in range(PIECES):
                piece(q, e0)
            sp.wait_ge(rt_scattered, 16 * TOPK * NT)
            sp.dma_start(rowslot, rowslot_dram.rearrange("(b p) a -> p (b a)", p=P),
                         allow_slow_non_contiguous=True).then_inc(d_rowslot, 16)
            with sp.Fori(0, MAXU - 1) as u:
                cls = sp.value_load(tab[0:1, ds(u * 4 + 4, 1)], min_val=0, max_val=NCLS)
                with sp.If(cls > 0):
                    e = sp.value_load(tab[0:1, ds(u * 4 + 5, 1)], min_val=0, max_val=NE - 1)
                    for q in range(PIECES):
                        sp.wait_ge(w_used, PIECES * u + q + 1)
                        piece(q, e)
            nunits = sp.value_load(tab[0:1, 3:4], min_val=1, max_val=MAXU)
            sp.wait_ge(w_used, nunits * PIECES)
            for i, v in enumerate((ln2_g, ln2_b)):
                sp.dma_start(ln2r[:, i], v.partition_broadcast(P).rearrange("p a n -> p (a n)")).then_inc(d_ln2, 16)
            sp.wait_ge(y_stored, nunits * 32)
            for t in range(NT):
                if t >= 1:
                    sp.wait_ge(yr_used, t)
                for T in ((0, 1) if t == 0 else (t + 1,)):
                    if T < NT:
                        sp.dma_start(yrows[T % 2], y_dram.rearrange("(k t p) n -> t p k n", k=TOPK, p=P)[T]).then_inc(d_yr[T % 2], 16)
                sp.wait_ge(fin_ready, t + 1)
                sp.dma_start(out[0, t * P:(t + 1) * P, :], fin[:, t % 2]).then_inc(fin_stored[t % 2], 16)
            sp.wait_ge(fin_stored[0], 16 * (NT // 2))
            sp.wait_ge(fin_stored[1], 16 * (NT // 2))

        def expert_unit(pe, u, v):
            n, nb = STEP * v, (STEP * v + P - 1) // P
            pe.wait_ge(xg_ready, 32 * u + 32)
            for k in range(KD):
                for b in range(nb):
                    mm = pe.transpose(ps[4 + k // 2][:, (k % 2) * WU + b * P:(k % 2) * WU + (b + 1) * P],
                                      xg[:, b, k * P:(k + 1) * P], ident[:, :])
            mm.then_inc(mx_turned, 1)
            pe.wait_ge(xT_act, u + 1)
            pe.wait_ge(xT_dve, u + 1)
            with pe.If(u > 0):
                pe.wait_ge(y_act, u)
                pe.wait_ge(y_dve, u)
            pe.nop()
            for g in range(2):
                for q in range(4):
                    pe.wait_ge(d_w[4 * g + q], 16 * u + 16)
                    for k in (2 * q, 2 * q + 1):
                        for m in range(KD):
                            mm = pe.matmul(ps[4 * g + m // 2][:, (m % 2) * WU:(m % 2) * WU + n],
                                           ring[4 * g + q][:, k % 2, m * P:(m + 1) * P], xT[:, k, 0:n],
                                           start=(k == 0 and m % 2 == 0), stop=(k == KD - 1), skip_group_check=True)
                    mm.then_inc(w_used, 1)
            for q in range(4):
                pe.wait_ge(d_w[8 + q], 16 * u + 16)
                for k in (2 * q, 2 * q + 1):
                    pe.wait_ge(act_ready, 8 * u + k + 1)
                    for b in range(nb):
                        for s in range(2):
                            mm = pe.matmul(ps[2 * b + s][:, :], act_[:, k, b * P:(b + 1) * P],
                                           ring[8 + q][:, k % 2, s * BANK:(s + 1) * BANK],
                                           start=(k == 0), stop=(k == KD - 1))
                mm.then_inc(w_used, 1)

        @block.tensor
        def _(pe):
            pe.wait_ge(const_ready, 1)
            pe.wait_ge(d_par, 16 * 10)
            pe.transpose(ps[0][:, 0:NPAR], prow[0:NPAR, :], ident[0:NPAR, 0:NPAR]).then_inc(par_turned, 1)
            pe.wait_ge(cs_ready, 1)
            for j in range(4):
                pe.wait_ge(d_wada[j % 3], 16 * (j // 3 + 1))
                for m in range(4):
                    q = 4 * j + m
                    for k in range(KD):
                        mm = pe.matmul(ps[1][:, 2 * q:2 * q + 2], wada_ring[:, j % 3, k, m * P:(m + 1) * P],
                                       csil[:, k, :], start=(k == 0), stop=(k == KD - 1))
                mm.then_inc(ada_used, 1)
            n = 0
            for grp, (t0, t1) in enumerate(((0, 4), (4, 8), (8, 10))):
                pe.wait_ge(d_x[grp], 16)
                for k in range(KD):
                    if n >= 4:
                        pe.wait_ge((uT_act, uT_dve)[n % 2], (n - 4) // 2 + 1)
                    for i, t in enumerate(range(t0, t1)):
                        mm = pe.transpose(ps[4 + n % 4][:, i * P:(i + 1) * P], xin[:, t, k * P:(k + 1) * P], ident[:, :])
                    mm.then_inc(x_turned, 1)
                    n += 1
            pe.wait_ge(csb_ready, 1)
            for j in range(4, 12):
                pe.wait_ge(d_wada[j % 3], 16 * (j // 3 + 1))
                if j >= 6:
                    pe.wait_ge(adarow_done, j - 5)
                for k in range(KD):
                    mm = pe.matmul(ps[2 + j % 2][:, :], csb[:, k, :], wada_ring[:, j % 3, k, :],
                                   start=(k == 0), stop=(k == KD - 1))
                mm.then_inc(ada_used, 1)
            pe.wait_ge(uT_act, 12)
            pe.wait_ge(uT_dve, 12)
            pe.wait_ge(adarow_done, 8)
            pe.wait_ge(d_wv, 16)

            def moving(kind, k, seg):
                if kind == "conv" and seg[0] < SEQ:
                    return colmajor(uT[:, k, 0:SEQ], seg[0] // GRID_W, 8)
                return uT[:, k, seg[0]:seg[1]]

            for i, (kind, j, seg, n) in enumerate(jobs):
                if i >= 8:
                    e, cnt = freed[i - 8]
                    pe.wait_ge((proj_act, proj_dve)[e], cnt)
                if kind == "v":
                    for k in range(KD):
                        mm = pe.matmul(ps[i % 8][:, :], uT[:, k, j * P:(j + 1) * P], wv[:, k, :], start=(k == 0), stop=(k == KD - 1))
                else:
                    w = tiles[n][3]
                    if i == 0 or jobs[i - 1][3] != n:
                        pe.wait_ge(d_win[n % WRING], 16 * (n // WRING + 1))
                    for k in range(KD):
                        mm = pe.matmul(ps[i % 8][0:w, 0:seg[1] - seg[0]], wring[n % WRING][:, k, 0:w],
                                       moving(kind, k, seg), start=(k == 0), stop=(k == KD - 1))
                mm.then_inc(proj_done, 1)
            pe.wait_ge(d_lruw, 16 * 8)
            pe.wait_ge(proj_dve, NPV)
            pe.wait_ge(proj_act, NPA)
            i = 0
            for d in range(2):
                for g in range(2):
                    for j in range(JL):
                        for s0, s1 in segs_all:
                            if i >= 8:
                                pe.wait_ge(lru_sig, i - 7)
                            pe.matmul(ps[i % 8][:, 0:s1 - s0], lruw[:, (d * 2 + g) * JL + j, :], XL[:, j, s0:s1],
                                      start=True, stop=True).then_inc(lru_mm, 1)
                            i += 1
            pe.wait_ge(lru_sig, i)
            pe.wait_ge(d_small, 16)
            nz = 0
            for pr in range(PAIRS):
                if pr:
                    pe.wait_ge(rms_act, 4 * pr)
                    pe.wait_ge(o_ready, NT * pr)
                for d in range(2):
                    for s0, s1 in segs_all:
                        if d:
                            pe.wait_ge(z_min, 6 * pr + nz % 6 - 2)
                            pe.wait_ge(z_abs, 6 * pr + nz % 6 - 2)
                        pe.matmul(ps[nz % 3][:, 0:s1 - s0], wa_sb[:, d, pr * P:(pr + 1) * P], AL[0:RANK, s0:s1],
                                  start=True, stop=True).then_inc(z_mm, 1)
                        nz += 1
                pe.wait_ge(z_min, 6 * pr + 6)
                pe.wait_ge(z_abs, 6 * pr + 6)
                for d in range(2):
                    pe.wait_ge(q_done, 2 * pr + d + 1)
                    for b, (t0, t1) in enumerate(((0, 4), (4, 8), (8, 10))):
                        for t in range(t0, t1):
                            mm = pe.transpose(ps[3 * d + b][:, (t - t0) * P:(t - t0 + 1) * P],
                                              gKE[:, d, t * P:(t + 1) * P], ident[:, :])
                        mm.then_inc(ke_turned, 1)
                pe.wait_ge(ke_ready, 6 * (pr + 1))
                for n in range(NS - 1):
                    for d in range(2):
                        ch = order[d][n]
                        T, h = ch // 2, ch % 2
                        if n >= 4:
                            pe.wait_ge(s_ready, 2 * (pr * 2 * (NS - 1) + 2 * (n - 4) + d + 1))
                        pe.matmul(ps[4 * d + n % 4][:, 0:2 * DV], gKT[64 * h:64 * h + 64, d, T, :],
                                  V[64 * h:64 * h + 64, T, 2 * pr * DV:(2 * pr + 2) * DV],
                                  start=True, stop=True).then_inc(kv_mm, 1)
                pe.wait_ge(s_ready, 4 * (pr + 1) * (NS - 1))

                def scores(T):
                    if T >= 2:
                        pe.wait_ge(sc_ready, 4 * (NT * pr + T - 1))
                    for d in range(2):
                        for h in range(2):
                            mm = pe.matmul(ps[2 * (T % 2) + h][:, d * P:(d + 1) * P],
                                           gK[64 * h:64 * h + 64, d, T * P:(T + 1) * P],
                                           gQ[64 * h:64 * h + 64, d, T * P:(T + 1) * P], start=True, stop=True)
                            mm.then_inc(sc_mm, 1)

                scores(0)
                for T in range(NT):
                    if T + 1 < NT:
                        scores(T + 1)
                    pe.wait_ge(sc_ready, 4 * (NT * pr + T + 1))
                    if T >= 2:
                        pe.wait_ge(o_ready, NT * pr + T - 1)
                    for h in range(2):
                        o_ = ps[4 + T % 2][:, h * P:(h + 1) * P]
                        vh = V[:, T, (2 * pr + h) * DV:(2 * pr + h + 1) * DV]
                        pe.matmul(o_, vh, gSc[:, T % 2, h, 0, :], start=True, stop=False, skip_group_check=True)
                        pe.matmul(o_, vh, gSc[:, T % 2, h, 1, :], start=False, stop=False, skip_group_check=True)
                        for cc in range(2):
                            for d in range(2):
                                ch = 2 * T + cc
                                mm = pe.matmul(o_[:, cc * CH:(cc + 1) * CH], gS[:, d, slot(order[d].index(ch)), h, :],
                                               gQ[:, d, ch * CH:(ch + 1) * CH], start=False,
                                               stop=(cc == 1 and d == 1), skip_group_check=True)
                    mm.then_inc(o_mm, 1)
                for h in range(2):
                    pe.wait_ge(sq_ready, 2 * pr + h + 1)
                    for s in range(2):
                        pe.matmul(ps[6 + s][:, :], ones[:, :], gSq[:, h, s * BANK:(s + 1) * BANK],
                                  start=True, stop=True).then_inc(rms_mm, 1)
                    if h == 0:
                        pe.wait_ge(rms_act, 4 * pr + 2)
            pe.wait_ge(gla_done, 4)
            pe.wait_ge(rms_act, 8)
            pe.wait_ge(lru_done, 2 * JL)
            pe.wait_ge(d_wout, 16)
            pe.wait_ge(d_rt, 64)
            for t in range(NT + 1):
                if t < NT:
                    if t >= 2:
                        pe.wait_ge(y_gated, 2 * (t - 1))
                    for s in range(2):
                        for k in range(KD):
                            mm = pe.matmul(ps[2 * (t % 2) + s][:, :], YT[:, k, t * P:(t + 1) * P],
                                           wout[:, k, s * BANK:(s + 1) * BANK], start=(k == 0), stop=(k == KD - 1))
                        mm.then_inc(out_mm, 1)
                if t >= 1:
                    T = t - 1
                    pe.wait_ge(h2_ready, T + 1)
                    if T >= 1:
                        pe.wait_ge(h2T_ready, 2 * T)
                    for k in range(KD):
                        mm = pe.transpose(ps[4 + k // 4][:, (k % 4) * P:(k % 4 + 1) * P],
                                          h2b[:, T % 2, k * P:(k + 1) * P], ident[:, :])
                        if k % 4 == 3:
                            mm.then_inc(h2_turned, 1)
                    pe.wait_ge(h2T_ready, 2 * T + 2)
                    for k in range(KD):
                        mm = pe.matmul(ps[6][:, T * NE:(T + 1) * NE], h2T[:, k, :], wrt[:, k, :],
                                       start=(k == 0), stop=(k == KD - 1))
                    mm.then_inc(logit_mm, 1)
            for g in range(2):
                for k in range(KD):
                    mm = pe.transpose(ps[7][:, (g * KD + k) * NE:(g * KD + k + 1) * NE],
                                      brow[0:NE, g, k * P:(k + 1) * P], ident[0:NE, 0:NE])
            mm.then_inc(bias_turned, 1)
            pe.wait_ge(sel_ready, 1)
            for T in range(NT):
                for s in range(T):
                    pe.matmul(ps[0][:, T * NE:(T + 1) * NE], ones[:, :], Mx[:, s, :], start=(s == 0), stop=False)
                pe.matmul(ps[0][:, T * NE:(T + 1) * NE], tri[:, :], Mx[:, T, :], start=(T == 0), stop=True)
            for T in range(NT):
                mm = pe.matmul(ps[1][:, 0:NE], ones[:, :], Mx[:, T, :], start=(T == 0), stop=(T == NT - 1))
            mm.then_inc(rank_mm, 1)
            pe.wait_ge(d_bdn, 16)
            pe.wait_ge(wd_ready, 1)
            for T in range(NT):
                if T:
                    pe.wait_ge(wdT_ready, T)
                pe.transpose(ps[6][0:NE, 0:P], Wd[:, T, :], ident[:, :]).then_inc(wd_turned, 1)
                pe.wait_ge(wdT_ready, T + 1)
                if T:
                    pe.wait_ge(bd_used, 2 * T)
                for s in range(2):
                    pe.matmul(ps[2 + s][:, :], WdT[0:NE, :], bdn[0:NE, 0, s * BANK:(s + 1) * BANK],
                              start=True, stop=True).then_inc(bd_mm, 1)
            pe.wait_ge(bias_ready, 1)
            pe.wait_ge(dest_ready, 1)
            pe.wait_ge(bd_used, 2 * NT)
            pe.wait_ge(tab_ready, 16)
            with pe.Fori(0, MAXU) as u:
                cls = pe.value_load(tab[0:1, ds(u * 4, 1)], min_val=0, max_val=NCLS)
                with pe.If(cls > 0):
                    for v in CLASSES:
                        with pe.If(cls == v):
                            expert_unit(pe, u, v)
                        pe.nop()

        @block.scalar
        def _(act):
            ch = Chain(act, ach)
            act.wait_ge(par_ready, 1)
            act.activation(csil[:, :, :], par[:, 0:2 * KD].rearrange("p (a k) -> p k a", a=2), ACT.Silu).then_inc(cs_ready, 1)
            act.wait_ge(par_ready, 2)
            act.activation(small[:, 0:8], small[:, 0:8], ACT.Exp, scale=-1.0).then_inc(cs_ready, 1)
            act.wait_ge(ada1_ready, 1)
            for n in range(0, 24, 2):
                grp, k = n // 8, n % 8
                w, c0, who = (512, 512 * grp, 0) if grp < 2 else (256, 1024, 1)
                act.wait_ge(x_turned, n + 1)
                act.activation(uT_out(n), uT_in(n), ACT.Identity,
                               bias=ada1[:, 0, k, who:who + 1], scale=ada1[:, 1, k, who:who + 1]).then_inc(uT_act, 1)
            nconv = 0
            for i, (kind, j, seg, n) in enumerate(jobs):
                if kind == "conv":
                    act.wait_ge(proj_done, i + 1)
                    act.activation(XL[:, j, seg[0]:seg[1]], ps[i % 8][:, 0:seg[1] - seg[0]], ACT.Identity,
                                   bias=par[:, C_CONVB + j:C_CONVB + j + 1],
                                   scale=par[:, C_CONVW + 2 * JL + j:C_CONVW + 2 * JL + j + 1]).then_inc(conv_started, 1)
                elif by_act[i]:
                    act.wait_ge(proj_done, i + 1)
                    if kind == "v":
                        act.copy(V[:, j, :], ps[i % 8][:, :]).then_inc(proj_act, 1)
                    elif kind == "gate":
                        act.activation(grid_half(YT[:, j], seg), half(ps[i % 8]), ACT.Gelu_apprx_tanh).then_inc(proj_act, 1)
                    else:
                        act.activation(grid_half(YT[:, JL + j], seg), half(ps[i % 8]), ACT.Silu).then_inc(proj_act, 1)
            i = 0
            act.wait_ge(cl_ready, 2)
            act.wait_ge(proj_act, NPA)
            for d in range(2):
                if d:
                    act.wait_ge(lru_done, JL)
                for g in range(2):
                    for j in range(JL):
                        for s0, s1 in segs_all:
                            act.wait_ge(lru_mm, i + 1)
                            bias = par[:, (C_BA, C_BX)[g] + d * JL + j:(C_BA, C_BX)[g] + d * JL + j + 1]
                            act.activation((lB, lC)[g][:, j, s0:s1], ps[i % 8][:, 0:s1 - s0], ACT.Sigmoid,
                                           bias=bias).then_inc(lru_sig, 1)
                            i += 1
                act.wait_ge(lru_sig, i)
                for j in range(JL):
                    act.activation(lA[:, j], lB[:, j], ACT.Exp, scale=cl[:, d * JL + j:d * JL + j + 1]).then_inc(lru_exp, 1)
                for j in range(JL):
                    act.activation(lB[:, j], lB[:, j], ACT.Tanh, scale=ncl[:, d * JL + j:d * JL + j + 1]).then_inc(lru_exp, 1)
                for j in range(JL):
                    act.wait_ge(lru_b2, d * JL + j + 1)
                    act.activation(lB[:, j], lB[:, j], ACT.Sqrt).then_inc(lru_sqrt, 1)
            nz = 0
            act.wait_ge(gmask_ready, 2)
            for pr in range(PAIRS):
                for d in range(2):
                    if pr + d:
                        act.wait_ge(q_done, 2 * pr + d)
                    gbias = par[:, C_GBA + d * PAIRS + pr:C_GBA + d * PAIRS + pr + 1]
                    for s0, s1 in segs_all:
                        act.wait_ge(z_mm, nz + 1)
                        act.activation(gE[:, s0:s1], ps[nz % 3][:, 0:s1 - s0], ACT.Abs, bias=gbias).then_inc(z_abs, 1)
                        nz += 1
                    act.wait_ge(z_abs, nz)
                    ch.link(act.activation(gE, gE, ACT.Exp, scale=-1.0))
                    act.activation(gE, gE, ACT.Ln, bias=1.0).then_inc(z_ln, 1)
                    act.wait_ge(cum_done, 3 * (2 * pr + d) + 1)
                    for m, sc in ((0, 1.0), (1, -1.0)):
                        if m:
                            act.wait_ge(eq_dve, 2 * (2 * pr + d) + 1)
                        act.activation(gE[:, 0:SEQ], gBC[:, d, 0:SEQ], ACT.Exp, scale=sc / 16).then_inc(eq_act, 1)
                    act.wait_ge(cum_done, 3 * (2 * pr + d) + 3)
                    act.activation(gKE[:, d], gKE[:, d], ACT.Exp, scale=1.0 / 16).then_inc(eq_act, 1)
                    act.activation(small[:, 0:NS] if d == 0 else small[:, 20:20 + NS],
                                   small[:, 0:NS] if d == 0 else small[:, 20:20 + NS], ACT.Exp,
                                   scale=1.0 / 16).then_inc(eq_act, 1)
                for b in range(6):
                    act.wait_ge(ke_turned, 6 * pr + b + 1)
                    w = 512 if b % 3 < 2 else 256
                    act.copy(gKT[:, b // 3, 4 * (b % 3):4 * (b % 3) + w // P, :],
                             ps[b][:, 0:w].rearrange("p (a b) -> p a b", b=P)).then_inc(ke_ready, 1)
                for T in range(NT):
                    act.wait_ge(o_mm, NT * pr + T + 1)
                    act.copy(gO[:, :, T * P:(T + 1) * P],
                             ps[4 + T % 2][:, 0:2 * P].rearrange("p (h b) -> p h b", h=2)).then_inc(o_ready, 1)
                act.wait_ge(o_ready, NT * (pr + 1))
                for h in range(2):
                    act.activation(gSq[:, h], gO[:, h], ACT.Square).then_inc(sq_ready, 1)
                for h in range(2):
                    for s in range(2):
                        act.wait_ge(rms_mm, 4 * pr + 2 * h + s + 1)
                        act.activation(gSq[:, h, s * BANK:(s + 1) * BANK], ps[6 + s][:, :], ACT.Sqrt,
                                       scale=1.0 / DV, bias=eps_rms[:, :]).then_inc(rms_act, 1)
            def std(n):
                act.wait_ge(var_ready, n + 1)
                act.activation(small[:, 48:49], small[:, 13:14], ACT.Sqrt, bias=eps_ln[:, :]).then_inc(std_ready, 1)

            std(0)
            for T in range(NT):
                if T + 1 < NT:
                    std(T + 1)
                for b in range(2):
                    act.wait_ge(h2_turned, 2 * T + b + 1)
                    if b == 0 and T:
                        act.wait_ge(logit_mm, T)
                    act.copy(h2T[:, 4 * b:4 * b + 4, :], ps[4 + b][:, :].rearrange("p (a b) -> p a b", b=P)).then_inc(h2T_ready, 1)
            act.wait_ge(top_exp_in, 1)
            act.activation(ev, ev, ACT.Exp).then_inc(top_exp, 1)
            for T in range(NT):
                act.wait_ge(wd_turned, T + 1)
                if T == 0:
                    act.wait_ge(logit_mm, NT)
                if T:
                    act.wait_ge(bd_mm, 2 * T)
                act.copy(WdT[0:NE, :], ps[6][0:NE, 0:P]).then_inc(wdT_ready, 1)
            act.wait_ge(tab_ready, 16)
            with act.Fori(0, MAXU) as u:
                cls = act.value_load(tab[0:1, ds(u * 4, 1)], min_val=0, max_val=NCLS)
                with act.If(cls > 0):
                    for v in CLASSES:
                        with act.If(cls == v):
                            n, nb = STEP * v, (STEP * v + P - 1) // P
                            act.wait_ge(mx_turned, u + 1)
                            act.copy(xT[:, 0:2, 0:nb * P], ps[4].rearrange("p (k n) -> p k n", k=2)[:, :, 0:nb * P])
                            act.copy(xT[:, 2:4, 0:nb * P], ps[5].rearrange("p (k n) -> p k n", k=2)[:, :, 0:nb * P]).then_inc(xT_act, 1)
                            for m in range(0, KD, 2):
                                act.wait_ge(g_ready, 8 * u + m + 2)
                                act.activation(sg[:, m:m + 2, 0:n], gb[:, m:m + 2, 0:n], ACT.Sigmoid,
                                               scale=SWIGLU).then_inc(sg_ready, 1)
                            act.wait_ge(w_used, PIECES * u + PIECES)
                            settle(act)
                            with act.If(u > 0):
                                act.wait_ge(y_stored, 32 * u)
                                settle(act)
                            act.nop()
                            for b in range(nb):
                                mm = act.copy(yb[:, b, 0:BANK], ps[2 * b][:, :])
                            mm.then_inc(y_act, 1)
                        act.nop()
            for T in range(NT):
                act.wait_ge(d_yr[T % 2], 16 * (T // 2 + 1))
                act.activation(acc[:, T % 2], yrows[T % 2][:, 0], ACT.Copy, scale=topw[:, T, 0:1]).then_inc(y0_scaled, 1)
                std(NT + T)
                act.wait_ge(xn_in, T + 1)
                if T >= 2:
                    act.wait_ge(fin_stored[T % 2], 16 * (T // 2))
                act.activation(fin[:, T % 2], acc[:, T % 2], ACT.Identity, bias=small[:, 50:51],
                               scale=small[:, 49:50]).then_inc(xn_ready, 1)

        @block.vector
        def _(dve):
            ch = Chain(dve, vch)
            link = ch.link
            dve.wait_ge(par_turned, 1)
            link(dve.tensor_copy(par[:, :], ps[0][:, 0:NPAR]))
            dve.nop().then_inc(par_ready, 1)
            link(dve.tensor_scalar(small[:, 8:16], par[:, C_LAM:C_LAM + 8], -1.0, None, ALU.mult))
            link(dve.tensor_tensor(small[:, 0:8], small[:, 8:16], par[:, C_LAM:C_LAM + 8], ALU.max))
            link(dve.tensor_scalar(small[:, 8:16], small[:, 8:16], 0.0, None, ALU.max))
            dve.nop().then_inc(par_ready, 1)
            dve.wait_ge(cs_ready, 2)
            link(dve.tensor_scalar(small[:, 16:24], small[:, 0:8], 2.0, None, ALU.add))
            link(dve.reciprocal(small[:, 16:24], small[:, 16:24]))
            link(dve.tensor_tensor(small[:, 16:24], small[:, 16:24], small[:, 0:8], ALU.mult))
            link(dve.tensor_tensor(small[:, 24:32], small[:, 16:24], small[:, 16:24], ALU.mult))
            link(dve.tensor_scalar(small[:, 0:8], small[:, 24:32], 1.0 / 15, 1.0 / 13, ALU.mult, ALU.add))
            for q in (11, 9, 7, 5, 3, 1):
                link(dve.tensor_tensor(small[:, 0:8], small[:, 0:8], small[:, 24:32], ALU.mult))
                link(dve.tensor_scalar(small[:, 0:8], small[:, 0:8], 1.0 / q, None, ALU.add))
            link(dve.tensor_tensor(small[:, 0:8], small[:, 0:8], small[:, 16:24], ALU.mult))
            link(dve.scalar_tensor_tensor(out=small[:, 0:8], in0=small[:, 0:8], scalar=2.0, in1=small[:, 8:16],
                                          op0=ALU.mult, op1=ALU.add))
            dve.tensor_scalar(cl[:, :], small[:, 0:8], -8.0, None, ALU.mult).then_inc(cl_ready, 1)
            dve.tensor_scalar(ncl[:, :], small[:, 0:8], 8.0, None, ALU.mult).then_inc(cl_ready, 1)
            dve.tensor_copy(csb, csil[:, :, 0:1].to_broadcast([P, KD, P])).then_inc(csb_ready, 1)
            dve.wait_ge(ada_used, 4)
            pada = ps[1][:, 0:4 * KD].rearrange("p (s k a) -> p s k a", s=2, a=2)
            for a in range(2):
                mm = dve.tensor_tensor(ada1[:, :, :, a], pada[:, :, :, a],
                                       par[:, C_BADA:C_BADA + 2 * KD].rearrange("p (s k) -> p s k", s=2), ALU.add)
                link(mm)
            dve.tensor_scalar(ada1[:, 1], ada1[:, 1], 1.0, None, ALU.add).then_inc(ada1_ready, 1)
            dve.wait_ge(ada1_ready, 1)
            for n in range(1, 24, 2):
                grp, k = n // 8, n % 8
                w, c0, who = (512, 512 * grp, 0) if grp < 2 else (256, 1024, 1)
                dve.wait_ge(x_turned, n + 1)
                dve.tensor_scalar(uT_out(n), uT_in(n), ada1[:, 1, k, who:who + 1],
                                  ada1[:, 0, k, who:who + 1], ALU.mult, ALU.add).then_inc(uT_dve, 1)
            dve.wait_ge(d_bada, 16)
            arow = adarow[:, :, :].rearrange("p a b -> p (a b)")
            for j in range(4, 12):
                dve.wait_ge(ada_used, j + 1)
                q = slice((j - 4) * 512, (j - 3) * 512)
                dve.tensor_tensor(arow[:, q], ps[2 + j % 2][:, :], arow[:, q], ALU.add).then_inc(adarow_done, 1)
            dve.wait_ge(adarow_done, 8)
            link(dve.tensor_scalar(adarow[:, 2], adarow[:, 2], 1.0, None, ALU.add))
            nconv = 0
            for i, (kind, j, seg, n) in enumerate(jobs):
                if by_act[i]:
                    continue
                src = ps[i % 8]
                if kind == "conv":
                    nconv += 1
                    dve.wait_ge(conv_started, nconv)
                    s0, s1 = seg
                    rw = GRID_W if s0 < SEQ else CTX
                    o3 = XL[:, j, s0:s1].rearrange("p (r w) -> p r w", w=rw)
                    i3 = src[:, 0:s1 - s0].rearrange("p (r w) -> p r w", w=rw)
                    for tap, sh in ((0, -2), (1, -1), (3, 1)):
                        a, b = max(0, -sh), rw - max(0, sh)
                        wt = par[:, C_CONVW + tap * JL + j:C_CONVW + tap * JL + j + 1]
                        mm = dve.scalar_tensor_tensor(out=o3[:, :, a:b], in0=i3[:, :, a + sh:b + sh], scalar=wt,
                                                      in1=o3[:, :, a:b], op0=ALU.mult, op1=ALU.add)
                        if tap < 3:
                            link(mm)
                    mm.then_inc(proj_dve, 1)
                    continue
                dve.wait_ge(proj_done, i + 1)
                if kind == "v":
                    dve.tensor_copy(V[:, j, :], src[:, :]).then_inc(proj_dve, 1)
                elif kind == "alow":
                    s0, s1 = seg
                    dve.tensor_copy(AL[0:RANK, s0:s1], src[0:RANK, 0:s1 - s0]).then_inc(proj_dve, 1)
                else:
                    s0, s1 = seg
                    dst, scale = (QT, DK ** -0.5) if kind == "q" else (KT, 1.0)
                    dve.tensor_scalar(dst[:, j, s0:s1], src[:, 0:s1 - s0], scale, None, ALU.mult).then_inc(proj_dve, 1)
            dve.wait_ge(const_ready, 3)
            dve.wait_ge(proj_act, NPA)
            for d in range(2):
                for j in range(JL):
                    dve.wait_ge(lru_exp, d * 2 * JL + JL + j + 1)
                    if j:
                        dve.wait_ge(lru_b2, d * JL + j)
                    link(dve.tensor_tensor(lT, lA[:, j], lA[:, j], ALU.mult))
                    dve.scalar_tensor_tensor(out=lB[:, j], in0=lT, scalar=1.0, in1=lB[:, j], op0=ALU.add,
                                             op1=ALU.mult).then_inc(lru_b2, 1)
                for j in range(JL):
                    dve.wait_ge(lru_ix, d * JL + j + 1)
                    dve.wait_ge(lru_sqrt, d * JL + j + 1)
                    link(dve.tensor_tensor(lC[:, j], lC[:, j], lB[:, j], ALU.mult))
                    cs = slice(SEQ, L) if d == 0 else slice(L - 1, SEQ - 1, -1)
                    lat = slice(0, SEQ) if d == 0 else slice(SEQ - 1, None, -1)
                    hc = lT[:, SEQ:L] if d == 0 else lT[:, L - 1:SEQ - 1:-1]
                    link(dve.tensor_tensor_scan(hc, lA[:, j, cs], lC[:, j, cs], 0.0, ALU.mult, ALU.add))
                    last = lT[:, L - 1:L] if d == 0 else lT[:, SEQ:SEQ + 1]
                    if d == 0:
                        link(dve.tensor_tensor_scan(lH[:, j], lA[:, j, lat], lC[:, j, lat], last, ALU.mult, ALU.add))
                        dve.nop().then_inc(lru_done, 1)
                    else:
                        link(dve.tensor_tensor_scan(arena_rev(lT, SEQ), arena_rev(lA[:, j], SEQ), arena_rev(lC[:, j], SEQ), last,
                                                    ALU.mult, ALU.add))
                        link(dve.tensor_tensor(lH[:, j], lH[:, j], lT[:, 0:SEQ], ALU.add))
                        dve.tensor_tensor(YT[:, j], YT[:, j], lH[:, j], ALU.mult).then_inc(lru_done, 1)
            dve.wait_ge(lru_done, 2 * JL)
            link(dve.memset(gS, 0.0))
            link(dve.memset(gSc, 0.0))
            for d in range(2):
                link(dve.memset(gMask[d], 1.0))
                edge = gMask[d].rearrange("p (n c) -> p n c", c=CH)[:, :, (0, CH - 1)[d]:(0, CH - 1)[d] + 1]
                link(dve.memset(edge, 0.0))
                dve.nop().then_inc(gmask_ready, 1)
            nz = 0
            ns = 0
            for pr in range(PAIRS):
                for d in range(2):
                    gbias = par[:, C_GBA + d * PAIRS + pr:C_GBA + d * PAIRS + pr + 1]
                    g = 2 * pr + d
                    if pr:
                        dve.wait_ge(gla_done, 2)
                    for s0, s1 in segs_all:
                        dve.wait_ge(z_abs, nz + 1)
                        dve.tensor_scalar(gKE[:, d, s0:s1], ps[nz % 3][:, 0:s1 - s0], gbias, 0.0, ALU.add,
                                          ALU.min).then_inc(z_min, 1)
                        nz += 1
                    dve.wait_ge(z_min, nz)
                    dve.wait_ge(z_ln, g + 1)
                    link(dve.tensor_tensor(gKE[:, d], gKE[:, d], gE, ALU.subtract))
                    if d == 0:
                        link(dve.tensor_tensor_scan(gBC[:, 0], gMask[0], gKE[:, 0], 0.0, ALU.mult, ALU.add))
                    else:
                        link(dve.tensor_tensor_scan(arena_rev(gBC[:, 1], L), arena_rev(gMask[1], L),
                                                    arena_rev(gKE[:, 1], L), 0.0, ALU.mult, ALU.add))
                    dve.nop().then_inc(cum_done, 1)
                    bc3 = gBC[:, d].rearrange("p (n c) -> p n c", c=CH)
                    btot = bc3[:, :, CH - 1:CH] if d == 0 else bc3[:, :, 0:1]
                    ke3 = gKE[:, d].rearrange("p (n c) -> p n c", c=CH)
                    dcol = small[:, 20 * d:20 * d + NS]
                    dve.tensor_copy(dcol.unsqueeze(2), btot).then_inc(cum_done, 1)
                    dve.tensor_tensor(ke3, btot.to_broadcast([P, NS, CH]), bc3, ALU.subtract).then_inc(cum_done, 1)
                    dve.wait_ge(eq_act, 4 * g + 1)
                    dve.tensor_tensor(gQ[:, d], gE[:, 0:SEQ], QT[:, pr], ALU.mult).then_inc(eq_dve, 1)
                    dve.wait_ge(eq_act, 4 * g + 2)
                    dve.tensor_tensor(gK[:, d], gE[:, 0:SEQ], KT[:, pr, 0:SEQ], ALU.mult).then_inc(eq_dve, 1)
                    dve.wait_ge(eq_dve, 2 * g + 2)
                    dve.wait_ge(eq_act, 4 * g + 4)
                    dve.tensor_tensor(gKE[:, d], gKE[:, d], KT[:, pr], ALU.mult).then_inc(q_done, 1)
                for n in range(NS - 1):
                    for d in range(2):
                        chn = order[d][n]
                        dve.wait_ge(kv_mm, pr * 2 * (NS - 1) + 2 * n + d + 1)
                        if n:
                            dve.wait_ge(s_ready, 2 * (pr * 2 * (NS - 1) + 2 * (n - 1) + d + 1))
                        for h in range(2):
                            q = slice(64 * h, 64 * h + 64)
                            pk = ps[4 * d + n % 4][q, h * DV:(h + 1) * DV]
                            if n == 0:
                                dve.tensor_copy(gS[q, d, slot(1), h, :], pk).then_inc(s_ready, 1)
                            else:
                                dve.scalar_tensor_tensor(out=gS[q, d, slot(n + 1), h, :], in0=gS[q, d, slot(n), h, :],
                                                         scalar=small[q, 20 * d + chn:20 * d + chn + 1], in1=pk,
                                                         op0=ALU.mult, op1=ALU.add).then_inc(s_ready, 1)
                for T in range(NT):
                    if T >= 2:
                        dve.wait_ge(o_mm, NT * pr + T - 1)
                    for h in range(2):
                        dve.wait_ge(sc_mm, 4 * (NT * pr + T + 1))
                        for d in range(2):
                            dve.copy_predicated(gSc[:, T % 2, h, d, :], masks[:, d, :],
                                                ps[2 * (T % 2) + h][:, d * P:(d + 1) * P]).then_inc(sc_ready, 1)
                for h in range(2):
                    H = 2 * pr + h
                    dve.wait_ge(rms_act, 4 * pr + 2 * h + 2)
                    link(dve.reciprocal(gSq[:, h], gSq[:, h]))
                    link(dve.scalar_tensor_tensor(out=gO[:, h], in0=gO[:, h], scalar=par[:, C_GN + H:C_GN + H + 1],
                                                  in1=gSq[:, h], op0=ALU.mult, op1=ALU.mult))
                    yv = YT[:, JL + H].rearrange("p (r w) -> p r w", w=GRID_W)
                    ov = gO[:, h].rearrange("p (w r) -> p r w", r=ROWS)
                    dve.tensor_tensor(yv, yv, ov, ALU.mult).then_inc(gla_done, 1)
            dve.wait_ge(gla_done, 4)
            dve.wait_ge(d_ln1, 32)
            st, mv = small[:, 0:12], small[:, 12:14]

            nstat = [0]

            def stats(v):
                for s in range(2):
                    link(dve.bn_stats(st[:, 6 * s:6 * s + 6], v[:, s * BANK:(s + 1) * BANK]))
                link(dve.bn_aggr(mv, st))
                dve.nop().then_inc(var_ready, 1)
                nstat[0] += 1
                dve.wait_ge(std_ready, nstat[0])
                link(dve.reciprocal(small[:, 49:50], small[:, 48:49]))

            for t in range(NT):
                yv = ybuf[:, t % 2]
                if t >= 2:
                    dve.wait_ge(x1_ready, t - 1)
                for s in range(2):
                    q = slice(s * BANK, (s + 1) * BANK)
                    dve.wait_ge(out_mm, 2 * t + s + 1)
                    dve.tensor_tensor(yv[:, q], ps[2 * (t % 2) + s][:, :], adarow[:, 0, q], ALU.mult).then_inc(y_gated, 1)
                dve.wait_ge(y_gated, 2 * t + 2)
                dve.wait_ge(d_xres[t % 2], 16 * (t // 2 + 1))
                link(dve.scalar_tensor_tensor(out=yv, in0=xres[:, t % 2], scalar=ALPHA, in1=yv, op0=ALU.mult, op1=ALU.add))
                stats(yv)
                link(dve.tensor_scalar(yv, yv, mv[:, 0:1], small[:, 49:50], ALU.subtract, ALU.mult))
                link(dve.tensor_tensor(yv, yv, ln1r[:, 0], ALU.mult))
                dve.tensor_tensor(X1[:, t], yv, ln1r[:, 1], ALU.add).then_inc(x1_ready, 1)
            dve.wait_ge(logit_mm, NT)
            dve.wait_ge(iota_ready, 2)
            for b in range(2):
                dve.wait_ge(h2_stored[b], 8 * NT)
            link(dve.tensor_tensor(lgt, ps[6][:, 0:NT * NE].rearrange("p (t e) -> p t e", t=NT),
                                   brt.unsqueeze(1).to_broadcast([P, NT, NE]), ALU.add))
            for T in range(NT):
                link(dve.max(mx8[:, T], lgt[:, T]))
                link(dve.max_index(ix8[:, T], mx8[:, T], lgt[:, T]))
            link(dve.tensor_copy(iot, ioti2))
            link(dve.tensor_copy(ixf, ix8))
            for k in range(TOPK):
                link(dve.tensor_tensor(OH[:, k], iot.unsqueeze(1).to_broadcast([P, NT, NE]),
                                       ixf[:, :, k:k + 1].to_broadcast([P, NT, NE]), ALU.is_equal))
            link(dve.tensor_tensor(Mx, OH[:, 0], OH[:, 1], ALU.add))
            link(dve.tensor_tensor(Mx, Mx, OH[:, 2], ALU.add))
            link(dve.tensor_tensor(Mx, Mx, OH[:, 3], ALU.add))
            dve.nop().then_inc(sel_ready, 1)
            dve.tensor_tensor(ev, mx8[:, :, 0:TOPK], mx8[:, :, 0:1].to_broadcast([P, NT, TOPK]), ALU.subtract).then_inc(top_exp_in, 1)
            dve.wait_ge(top_exp, 1)
            sm, rc = small[:, 0:8], small[:, 8:16]
            link(dve.tensor_reduce(sm, ev, AX_X, ALU.add))
            link(dve.reciprocal(rc, sm))
            link(dve.tensor_tensor(topw, ev, rc.unsqueeze(2).to_broadcast([P, NT, TOPK]), ALU.mult))
            link(dve.tensor_tensor(Wd, OH[:, 0], topw[:, :, 0:1].to_broadcast([P, NT, NE]), ALU.mult))
            for k in range(1, TOPK):
                link(dve.tensor_tensor(tmpO, OH[:, k], topw[:, :, k:k + 1].to_broadcast([P, NT, NE]), ALU.mult))
                link(dve.tensor_tensor(Wd, Wd, tmpO, ALU.add))
            dve.nop().then_inc(wd_ready, 1)
            dve.wait_ge(rank_mm, 1)
            CNT, NB, IB, BASE, NU, IU, US, ON, T0, T1 = range(10)
            r = lambda i: rt[:, i]
            ri = lambda i: rt[:, i].bitcast(I32)
            link(dve.tensor_copy(r(CNT), ps[1][:, 0:NE]))
            link(dve.memset(r(ON), 1.0))

            def blocks(dst, cum, sh):
                link(dve.tensor_scalar(ri(T0), r(CNT), float((1 << sh) - 1), None, ALU.add))
                link(dve.tensor_scalar(ri(T1), ri(T0), sh, None, ALU.logical_shift_right))
                link(dve.tensor_copy(r(dst), ri(T1)))
                link(dve.tensor_tensor_scan(r(cum), r(ON), r(dst), 0.0, ALU.mult, ALU.add))

            blocks(NB, IB, 7)
            link(dve.tensor_tensor(r(BASE), r(IB), r(NB), ALU.subtract))
            link(dve.tensor_scalar(r(BASE), r(BASE), 128.0, None, ALU.mult))
            blocks(NU, IU, 8)
            link(dve.tensor_tensor(r(US), r(IU), r(NU), ALU.subtract))
            link(dve.tensor_tensor(Gx, ps[0][:, 0:NT * NE].rearrange("p (t e) -> p t e", t=NT),
                                   r(BASE).unsqueeze(1).to_broadcast([P, NT, NE]), ALU.add))
            for k in range(TOPK):
                link(dve.tensor_tensor(tmpO, OH[:, k], Gx, ALU.mult))
                link(dve.tensor_reduce(small[:, 0:8], tmpO, AX_X, ALU.add))
                link(dve.tensor_copy(dest[:, k], small[:, 0:8]))
            dve.nop().then_inc(dest_ready, 1)
            U = small[:, 16:32]
            uf = U[:, 0:1]
            link(dve.tensor_copy(uf, slotid[:, 0, 0:1]))
            link(dve.tensor_scalar(r(T0), r(IU), uf, None, ALU.is_le))
            link(dve.tensor_reduce(U[:, 1:2], r(T0), AX_X, ALU.add))
            link(dve.tensor_scalar(r(T0), iot, U[:, 1:2], None, ALU.is_equal))
            for i, src in enumerate((CNT, US, BASE)):
                link(dve.tensor_tensor(r(T1), r(T0), r(src), ALU.mult))
                link(dve.tensor_reduce(U[:, 2 + i:3 + i], r(T1), AX_X, ALU.add))
            link(dve.tensor_tensor(U[:, 5:6], uf, U[:, 3:4], ALU.subtract))
            link(dve.tensor_scalar(U[:, 5:6], U[:, 5:6], float(WU), None, ALU.mult))
            link(dve.tensor_tensor(U[:, 6:7], U[:, 2:3], U[:, 5:6], ALU.subtract))
            link(dve.tensor_scalar(U[:, 6:7], U[:, 6:7], 0.0, float(STEP - 1), ALU.max, ALU.add))
            link(dve.tensor_copy(U[:, 7:8].bitcast(I32), U[:, 6:7]))
            link(dve.tensor_scalar(U[:, 8:9].bitcast(I32), U[:, 7:8].bitcast(I32), 5, None, ALU.logical_shift_right))
            link(dve.tensor_scalar(U[:, 10:11], U[:, 8:9].bitcast(I32), float(P // STEP), float(NCLS), ALU.max, ALU.min))
            link(dve.tensor_scalar(U[:, 11:12], U[:, 6:7], float(STEP), None, ALU.is_ge))
            link(dve.tensor_tensor(tabc[:, 0:1], U[:, 10:11], U[:, 11:12], ALU.mult))
            link(dve.tensor_scalar(tabc[:, 1:2], U[:, 1:2], float(NE - 1), None, ALU.min))
            link(dve.tensor_tensor(U[:, 9:10], U[:, 4:5], U[:, 5:6], ALU.add))
            link(dve.tensor_scalar(tabc[:, 2:3], U[:, 9:10], 1.0 / P, float(BLOCKS - 2), ALU.mult, ALU.min))
            link(dve.tensor_copy(tabc[:, 3:4], r(IU)[:, NE - 1:NE]))
            dve.nop().then_inc(tab_col, 1)
            dve.wait_ge(bias_turned, 1)
            link(dve.tensor_copy(bgT, ps[7][:, 0:KD * NE].rearrange("p (k e) -> p k e", k=KD)))
            link(dve.tensor_scalar(buT, ps[7][:, KD * NE:2 * KD * NE].rearrange("p (k e) -> p k e", k=KD), 1.0, None, ALU.add))
            dve.nop().then_inc(bias_ready, 1)
            dve.wait_ge(x1_ready, NT)
            dve.wait_ge(h2_ready, NT)
            link(dve.tensor_scalar(X1, X1, ALPHA, None, ALU.mult))
            for T in range(NT):
                for s in range(2):
                    q = slice(s * BANK, (s + 1) * BANK)
                    dve.wait_ge(bd_mm, 2 * T + s + 1)
                    if T:
                        dve.wait_ge(bd_used, 2 * T + s - 1)
                    link(dve.tensor_tensor(xres[:, s, 0:BANK], ps[2 + s][:, :], adarow[:, 3, q], ALU.mult))
                    dve.tensor_tensor(X1[:, T, q], X1[:, T, q], xres[:, s, 0:BANK], ALU.add).then_inc(bd_used, 1)
            dve.wait_ge(bd_used, 2 * NT)
            dve.wait_ge(dest_ready, 1)
            link(dve.memset(act_, 0.0))
            link(dve.memset(yb, 0.0))
            dve.wait_ge(d_rowslot, 16)
            link(dve.tensor_scalar(rowtok, rowslot, SEQ - 1, None, ALU.bitwise_and))
            dve.nop().then_inc(moe_clear, 1)
            dve.wait_ge(tab_ready, 16)
            with dve.Fori(0, MAXU) as u:
                cls = dve.value_load(tab[0:1, ds(u * 4, 1)], min_val=0, max_val=NCLS)
                with dve.If(cls > 0):
                    e = dve.value_load(tab[0:1, ds(u * 4 + 1, 1)], min_val=0, max_val=NE - 1)
                    dve.tensor_copy(bgc.unsqueeze(2), bgT[:, :, ds(e, 1)]).then_inc(bias_now, 1)
                    dve.tensor_copy(buc.unsqueeze(2), buT[:, :, ds(e, 1)]).then_inc(bias_now, 1)
                    for v in CLASSES:
                        with dve.If(cls == v):
                            n, nb = STEP * v, (STEP * v + P - 1) // P
                            dve.wait_ge(mx_turned, u + 1)
                            dve.tensor_copy(xT[:, 4:6, 0:nb * P], ps[6].rearrange("p (k n) -> p k n", k=2)[:, :, 0:nb * P])
                            dve.tensor_copy(xT[:, 6:8, 0:nb * P], ps[7].rearrange("p (k n) -> p k n", k=2)[:, :, 0:nb * P]).then_inc(xT_dve, 1)
                            dve.wait_ge(bias_now, 2 * u + 2)
                            dve.wait_ge(w_used, PIECES * u + 4)
                            for m in range(KD):
                                dve.tensor_scalar(gb[:, m, 0:n], ps[m // 2][:, (m % 2) * WU:(m % 2) * WU + n],
                                                  bgc[:, m:m + 1], LIMIT, ALU.add, ALU.min).then_inc(g_ready, 1)
                            for m in range(0, KD, 2):
                                dve.wait_ge(sg_ready, 4 * u + m // 2 + 1)
                                dve.tensor_tensor(gb[:, m:m + 2, 0:n], gb[:, m:m + 2, 0:n], sg[:, m:m + 2, 0:n],
                                                  ALU.mult).then_inc(gs_ready, 1)
                            dve.wait_ge(gs_ready, 4 * u + 4)
                            dve.wait_ge(w_used, PIECES * u + 8)
                            for m in range(KD + 1):
                                if m < KD:
                                    dve.tensor_scalar(sg[:, m, 0:n], ps[4 + m // 2][:, (m % 2) * WU:(m % 2) * WU + n],
                                                      buc[:, m:m + 1], 1.0 - LIMIT, ALU.add, ALU.max).then_inc(t_ready, 1)
                                if m:
                                    dve.wait_ge(t_ready, 8 * u + m)
                                    dve.scalar_tensor_tensor(out=act_[:, m - 1, 0:n], in0=sg[:, m - 1, 0:n],
                                                             scalar=1.0 + LIMIT, in1=gb[:, m - 1, 0:n], op0=ALU.min,
                                                             op1=ALU.mult).then_inc(act_ready, 1)
                            dve.wait_ge(w_used, PIECES * u + PIECES)
                            settle(dve)
                            with dve.If(u > 0):
                                dve.wait_ge(y_stored, 32 * u)
                                settle(dve)
                            dve.nop()
                            for b in range(nb):
                                mm = dve.tensor_copy(yb[:, b, BANK:D], ps[2 * b + 1][:, :])
                            mm.then_inc(y_dve, 1)
                        dve.nop()
            dve.wait_ge(d_ln2, 32)
            for T in range(NT):
                a = acc[:, T % 2]
                if T:
                    dve.wait_ge(xn_ready, T)
                dve.wait_ge(y0_scaled, T + 1)
                for k in range(1, TOPK):
                    mm = dve.scalar_tensor_tensor(out=a, in0=yrows[T % 2][:, k], scalar=topw[:, T, k:k + 1], in1=a,
                                                  op0=ALU.mult, op1=ALU.add)
                    link(mm)
                dve.nop().then_inc(yr_used, 1)
                link(dve.tensor_tensor(a, a, adarow[:, 3], ALU.mult))
                link(dve.tensor_tensor(a, a, X1[:, T], ALU.add))
                stats(a)
                link(dve.scalar_tensor_tensor(out=small[:, 50:51], in0=mv[:, 0:1], scalar=-1.0, in1=small[:, 49:50],
                                              op0=ALU.mult, op1=ALU.mult))
                dve.nop().then_inc(xn_in, 1)

        @block.gpsimd
        def _(pool):
            ch = Chain(pool, pch)
            link = ch.link
            link(pool.memset(ident[:, :], 0.0))
            pool.affine_select(out=ident[:, :], in_=ident[:, :], compare_op=ALU.not_equal, fill=1.0, base=0,
                               pattern=[[-1, P]], channel_multiplier=1).then_inc(const_ready, 1)
            pool.memset(lruw[:, :, :], 0.0).then_inc(const_ready, 1)
            link(pool.memset(ones[:, :], 1.0))
            link(pool.memset(eps_ln[:, :], LN_EPS))
            link(pool.memset(eps_rms[:, :], RMS_EPS))
            link(pool.affine_select(out=tri[:, :], in_=ones[:, :], compare_op=ALU.is_gt, fill=0.0, base=0,
                                    pattern=[[1, P]], channel_multiplier=-1))
            mf = fmask
            for d in range(2):
                sgn = 1 - 2 * d
                link(pool.affine_select(out=mf, in_=ones[:, :], compare_op=ALU.is_ge, fill=0.0, base=0,
                                        pattern=[[sgn, P]], channel_multiplier=-sgn))
                if d == 0:
                    link(pool.memset(mf[0:CH, CH:P], 0.0))
                else:
                    link(pool.memset(mf[CH:P, 0:CH], 0.0))
                link(pool.tensor_copy(masks[:, d, :], mf))
            pool.nop().then_inc(const_ready, 1)
            for d in range(2):
                for j in range(JL):
                    pool.wait_ge(lru_sig, d * 6 * JL + 3 * JL + 3 * j + 3)
                    pool.tensor_tensor(lC[:, j], lC[:, j], XL[:, j], ALU.mult).then_inc(lru_ix, 1)
            for t in range(NT):
                pool.wait_ge(x1_ready, t + 1)
                if t >= 2:
                    pool.wait_ge(h2_stored[t % 2], 16 * (t // 2))
                    pool.wait_ge(h2_turned, 2 * (t - 1))
                link(pool.tensor_tensor(h2b[:, t % 2], X1[:, t], adarow[:, 2], ALU.mult))
                pool.tensor_tensor(h2b[:, t % 2], h2b[:, t % 2], adarow[:, 1], ALU.add).then_inc(h2_ready, 1)
            for b in range(2):
                pool.wait_ge(h2_stored[b], 8 * NT)
            pool.wait_ge(h2_turned, 2 * NT)
            pool.iota(slotid, pattern=[[SEQ, TOPK], [P, NT]], base=0, channel_multiplier=1).then_inc(iota_ready, 1)
            pool.iota(ioti2, pattern=[[1, NE]], base=0, channel_multiplier=0).then_inc(iota_ready, 1)
            link(pool.memset(rowslot, NOSLOT))
            pool.dma_start(rowslot_dram.rearrange("(p n) a -> p (n a)", p=P), rowslot).then_inc(rt_zeroed, 16)
            pool.wait_ge(rt_zeroed, 16)
            pool.wait_ge(dest_ready, 1)
            pool.wait_ge(iota_ready, 2)
            for k in range(TOPK):
                for T in range(NT):
                    pool.indirect_dma_start(out=rowslot_dram, out_offset=bass.IndirectOffsetOnAxis(ap=dest[:, k, T:T + 1], axis=0),
                                            in_=slotid[:, k, T:T + 1], in_offset=None).then_inc(rt_scattered, 16)

            def scatter(b):
                pool.indirect_dma_start(out=y_dram, out_offset=bass.IndirectOffsetOnAxis(ap=sidx[:, b:b + 1], axis=0),
                                        in_=yb[:, b], in_offset=None, bounds_check=TOPK * SEQ - 1,
                                        oob_is_err=False).then_inc(y_stored, 16)

            pool.wait_ge(tab_ready, 16)
            pool.wait_ge(moe_clear, 1)
            with pool.Fori(0, MAXU) as u:
                cls = pool.value_load(tab[0:1, ds(u * 4, 1)], min_val=0, max_val=NCLS)
                with pool.If(cls > 0):
                    blk = pool.value_load(tab[0:1, ds(u * 4 + 2, 1)], min_val=0, max_val=BLOCKS - 2)
                    with pool.If(u > 0):
                        pool.wait_ge(xg_ready, 32 * u)
                        pool.wait_ge(mx_turned, u)
                        settle(pool)
                    pool.tensor_copy(gidx.bitcast(I32), rowtok[:, ds(blk, 2)]).then_inc(gidx_ready, 1)
                    pool.wait_ge(gidx_ready, u + 1)
                    settle(pool)
                    for b in range(2):
                        pool.indirect_dma_start(out=xg[:, b], out_offset=None, in_=h2_dram,
                                                in_offset=bass.IndirectOffsetOnAxis(ap=gidx[:, b:b + 1], axis=0)).then_inc(xg_ready, 16)
                    with pool.If(u > 0):
                        pool.wait_ge(y_act, u)
                        settle(pool)
                        pool.wait_ge(y_dve, u)
                        settle(pool)
                        for b in range(2):
                            scatter(b)
                        pool.wait_ge(y_stored, 32 * u)
                    pool.tensor_copy(sidx.bitcast(I32), rowslot[:, ds(blk, 2)]).then_inc(sidx_ready, 1)
                    pool.wait_ge(sidx_ready, 2 * u + 1)
                    settle(pool)
                    with pool.If(cls <= NCLS // 2):
                        pool.memset(sidx.bitcast(I32)[:, 1:2], NOSLOT)
                    pool.nop()
                    pool.tensor_copy(sidx.bitcast(I32)[:, 0:1], sidx.bitcast(I32)[:, 0:1]).then_inc(sidx_ready, 1)
                    pool.wait_ge(sidx_ready, 2 * u + 2)
                    settle(pool)
            nunits = pool.value_load(tab[0:1, 3:4], min_val=1, max_val=MAXU)
            pool.wait_ge(y_act, nunits)
            settle(pool)
            pool.wait_ge(y_dve, nunits)
            settle(pool)
            for b in range(2):
                scatter(b)
            pool.wait_ge(d_ln2, 32)
            for T in range(NT):
                f = fin[:, T % 2]
                pool.wait_ge(xn_ready, T + 1)
                link(pool.tensor_tensor(f, f, ln2r[:, 0], ALU.mult))
                pool.tensor_tensor(f, f, ln2r[:, 1], ALU.add).then_inc(fin_ready, 1)


_INS = ['x', 'c', 'ctx', 'c_ctx', 'w_ada', 'b_ada', 'w_in', 'conv_w', 'conv_b', 'lru_wa', 'lru_ba', 'lru_wx', 'lru_bx',
        'lru_lam', 'gla_wa', 'gla_ba', 'gla_norm_g', 'w_out', 'ln1_g', 'ln1_b', 'w_router', 'b_router', 'w_gate',
        'b_gate', 'w_up', 'b_up', 'w_down', 'b_down', 'ln2_g', 'ln2_b']


def kernel(**inputs):
    import numpy as _np
    import concourse.bacc as _bacc
    from concourse import mybir as _mybir
    from concourse.bass_utils import run_bass_kernel_spmd as _run

    nc = _bacc.Bacc("TRN2", target_bir_lowering=False, num_devices=1)
    arrays, args = {}, []
    for name in _INS:
        a = _np.ascontiguousarray(inputs[name])
        arrays[f"in_{name}_dram"] = a
        args.append(nc.dram_tensor(f"in_{name}_dram", a.shape, _mybir.dt.from_np(a.dtype), kind="ExternalInput").ap())
    args.append(nc.dram_tensor("out_dram", inputs["x"].shape, _mybir.dt.float32, kind="ExternalOutput").ap())
    layer(nc, *args)
    r = _run(nc, [arrays], core_ids=[0])
    return r.results[0]["out_dram"]
```

```python
from contextlib import ExitStack

import concourse.bass as bass
from concourse import mybir

ALU = mybir.AluOpType
ACT = mybir.ActivationFunctionType
AX_X = mybir.AxisListType.X
F32 = mybir.dt.float32
I32 = mybir.dt.int32
U32 = mybir.dt.uint32

P = 128
BANK = 512
ds = bass.ds


class Chain:

    def __init__(self, eng, sem):
        self.eng, self.sem, self.n = eng, sem, 0

    def link(self, ins):
        self.n += 1
        ins.then_inc(self.sem, 1)
        self.eng.wait_ge(self.sem, self.n)


def layer(nc, x, c, ctx, c_ctx, w_ada, b_ada, w_in, conv_w, conv_b, lru_wa, lru_ba, lru_wx, lru_bx,
          lru_lam, gla_wa, gla_ba, gla_norm_g, w_out, ln1_g, ln1_b, w_router, b_router, w_gate,
          b_gate, w_up, b_up, w_down, b_down, ln2_g, ln2_b, out):
    SEQ, D = x.shape[1], x.shape[2]
    CTX = ctx.shape[1]
    L = SEQ + CTX
    GRID_W = 64
    ROWS = SEQ // GRID_W
    KD = D // P
    NT, NTC = SEQ // P, CTX // P
    D_LRU = conv_w.shape[2]
    JL = D_LRU // P
    DK, DV = 64, 128
    HEADS = (D - D_LRU) // DV
    PAIRS = HEADS // 2
    RANK = gla_wa.shape[2]
    CH = 64
    NCH, NCHC = SEQ // CH, CTX // CH
    NE, TOPK = w_router.shape[2], 4
    ALPHA = 2.0 ** 0.25
    LN_EPS, RMS_EPS = 1e-5, 1e-6
    LIMIT, SWIGLU = 7.0, 1.702
    WU = 256
    STEP = 32
    NCLS = WU // STEP
    CLASSES = range(P // STEP, NCLS + 1)
    MAXU = NE - 1 + SEQ * TOPK // WU
    PIECES = 12
    MAXROWS = SEQ * TOPK + NE * P
    BLOCKS = MAXROWS // P + 1
    NOSLOT = 1 << 20
    segs_all = [(0, 512), (512, 1024), (1024, L)]
    segs_lat = segs_all[:2]

    h2_dram = nc.dram_tensor("h2_rows", [SEQ, D], F32).ap()
    y_dram = nc.dram_tensor("expert_rows", [TOPK * SEQ, D], F32).ap()
    rowslot_dram = nc.dram_tensor("row_slot", [MAXROWS + P, 1], I32).ap()
    tab_dram = nc.dram_tensor("unit_table", [P, 4], I32).ap()

    ctxs = ExitStack()
    with ctxs:
        def sb(name, shape, dt=F32):
            return ctxs.enter_context(nc.sbuf_tensor(name, shape, dt))

        def sem(name):
            return ctxs.enter_context(nc.semaphore(name))

        ident = sb("ident", [P, P])
        ones = sb("ones", [P, P])
        tri = sb("tri", [P, P])
        masks = sb("masks", [P, 2, P], I32)
        par = sb("par", [P, 84])
        ada1 = sb("ada1", [P, 2, KD, 2])
        adarow = sb("adarow", [P, 4, D])
        lruw = sb("lruw", [P, 16, P])
        cl = sb("cl", [P, 2 * JL])
        ncl = sb("ncl", [P, 2 * JL])
        small = sb("small", [P, 64])
        tab = sb("tab", [1, 4 * P], I32)
        C_C, C_CTX, C_BADA, C_CONVW, C_CONVB = 0, 8, 16, 32, 48
        C_BA, C_BX, C_LAM, C_GBA, C_GN, NPAR = 52, 60, 68, 76, 80, 84

        AW = 45056
        arena = sb("arena", [P, AW])

        def reg(off, *shape):
            n = 1
            for s in shape:
                n *= s
            assert off + n <= AW
            v = arena[:, off:off + n]
            if len(shape) == 2:
                v = v.rearrange("p (a b) -> p a b", a=shape[0])
            if len(shape) == 3:
                v = v.rearrange("p (a b c) -> p a b c", a=shape[0], b=shape[1])
            if len(shape) == 4:
                v = v.rearrange("p (a b c d) -> p a b c d", a=shape[0], b=shape[1], c=shape[2])
            return v

        O_YT, O_XL, O_QT, O_KT, O_V, O_AL, O_R = 0, 8192, 13312, 15360, 17920, 23040, 24320
        YT = reg(O_YT, KD, SEQ)
        XL = reg(O_XL, JL, L)
        QT = reg(O_QT, PAIRS, SEQ)
        KT = reg(O_KT, PAIRS, L)
        V = reg(O_V, NT + NTC, HEADS * DV)
        AL = reg(O_AL, L)
        wada_ring = reg(0, 3, KD, 512)
        csb = reg(12288, KD, P)
        prow = reg(O_R, P)
        xin = reg(O_QT, NT + NTC, D)
        uT = reg(O_R, KD, L)
        wv = reg(O_R + 10240, KD, 512)
        WRING = 5
        wring = [reg(O_R + 15360 + 1024 * s, KD, P) for s in range(WRING)]
        lA, lB, lC, lT = (reg(O_R + 10240 + L * i, L) for i in range(4))
        lH = YT[:, 0:JL]
        gelu_ = reg(O_R + 10240, 2 * JL, BANK)
        O_G = O_XL
        gBC = reg(O_XL, 2, L)
        gE = reg(O_XL + 2560, L)
        gMask = [reg(O_XL + 3840, L), reg(O_R, L)]
        o = O_R + 1280
        gQ = reg(o, 2, SEQ); o += 2048
        gK = reg(o, 2, SEQ); o += 2048
        gKE = reg(o, 2, L); o += 2560
        gKT = reg(o, 2, NT + NTC, P); o += 2560
        NSLOT = 2 + NCH
        gS = reg(o, 2, NSLOT, 2, DV); o += 2 * NSLOT * 2 * DV
        gSc = reg(o, 2, 2, 2, P); o += 1024
        assert o <= AW
        gO = reg(O_XL, 2, SEQ)
        gSq = reg(O_R + 1280 + 4096, 2, SEQ)
        wout = reg(O_QT, KD, D)
        O_X1 = 24576
        X1 = reg(O_X1, NT, D)
        o = O_X1 + 8192
        xres = reg(o, 2, D); o += 2048
        ybuf = reg(o, 2, D); o += 2048
        h2b = reg(o, 2, D); o += 2048
        h2T = reg(o, KD, P); o += 1024
        ln1r = reg(o, 2, D); o += 2048
        wrt = reg(o, KD, NE); o += 256
        brow = reg(o, 2, D); o += 2048
        O_RT = o
        lgt = reg(O_RT, NT, NE)
        assert O_RT + 256 <= AW
        o = O_X1 + 8192 + 2048
        OH = reg(o, TOPK, NT, NE); o += 1024
        tmpO = reg(o, NT, NE); o += 256
        Mx = reg(o, NT, NE); o += 256
        Gx = reg(o, NT, NE); o += 256
        Wd = reg(o, NT, NE); o += 256
        mx8 = reg(o, NT, 8); o += 64
        ix8 = reg(o, NT, 8).bitcast(U32); o += 64
        ixf = reg(o, NT, 8); o += 64
        ev = reg(o, NT, TOPK); o += 32
        iot = reg(o, NE); o += 32
        rt = reg(o, 16, NE); o += 512
        assert o <= O_X1 + 8192 + 6144
        WdT = reg(O_RT - 2048 - 256 - 2048 - 1024, P)
        lw = lruw[:, :, :].rearrange("p a b -> p (a b)")
        bgT = lw[:, 0:256].rearrange("p (k e) -> p k e", k=KD)
        buT = lw[:, 256:512].rearrange("p (k e) -> p k e", k=KD)
        topw = lw[:, 512:544].rearrange("p (t k) -> p t k", t=NT)
        dest = lw[:, 544:576].bitcast(U32).rearrange("p (k t) -> p k t", k=TOPK)
        slotid = lw[:, 800:832].bitcast(I32).rearrange("p (k t) -> p k t", k=TOPK)
        bgc = lw[:, 592:600]
        buc = lw[:, 600:608]
        gidx = lw[:, 608:610].bitcast(U32)
        sidx = lw[:, 612:614].bitcast(U32)
        brt = lw[:, 640:672]
        ioti2 = lw[:, 672:704].bitcast(I32)
        wa_sb = lw[0:RANK, 1024:1536].rearrange("p (a b) -> p a b", a=2)
        tabc = small[:, 40:44].bitcast(I32)
        fmask = reg(AW - P, P)
        eps_ln, eps_rms = sb("eps_ln", [P, 1]), sb("eps_rms", [P, 1])
        csil = sb("csil", [P, KD, 2])
        rowslot = lw[:, 704:704 + BLOCKS].bitcast(I32)
        rowtok = lw[:, 896:896 + BLOCKS].bitcast(I32)
        bdn = reg(O_X1 + 8192 + 6144 + 1024, 1, D)
        ring = [reg(2048 * q, 2, D) for q in range(PIECES)]
        o = O_X1 + 8192
        xg = reg(o, 2, D); o += 2048
        xT = reg(o, KD, WU); o += 2048
        gb = reg(o, KD, WU); o += 2048
        sg = reg(o, KD, WU); o += 2048
        act_ = reg(o, KD, WU); o += 2048
        yb = reg(o, 2, D); o += 2048
        assert o <= AW
        yrows = [reg(TOPK * 1024 * b, TOPK, D) for b in range(2)]
        acc = reg(8192, 2, D)
        ln2r = reg(10240, 2, D)
        fin = reg(12288, 2, D)

        ps = [ctxs.enter_context(nc.psum_tensor(f"ps{i}", [P, BANK], F32)) for i in range(8)]

        settled = {e.engine: sem(f"settled{i}") for i, e in enumerate((nc.scalar, nc.vector, nc.gpsimd))}
        var_ready, std_ready = sem("var_ready"), sem("std_ready")
        vch, ach, pch = sem("vector_chain"), sem("scalar_chain"), sem("pool_chain")
        const_ready = sem("const_ready")
        d_par, d_lruw, d_bada, d_wv, d_small = sem("d_par"), sem("d_lruw"), sem("d_bada"), sem("d_wv"), sem("d_small")
        d_wada = [sem(f"d_wada{i}") for i in range(3)]
        d_x = [sem(f"d_x{i}") for i in range(3)]
        d_win = [sem(f"d_win{i}") for i in range(WRING)]
        par_turned, par_ready, cs_ready, csb_ready = sem("par_turned"), sem("par_ready"), sem("cs_ready"), sem("csb_ready")
        ada_used, ada1_ready, adarow_done = sem("ada_used"), sem("ada1_ready"), sem("adarow_done")
        x_turned, uT_act, uT_dve = sem("x_turned"), sem("uT_act"), sem("uT_dve")
        proj_done, proj_act, proj_dve, conv_started = sem("proj_done"), sem("proj_act"), sem("proj_dve"), sem("conv_started")
        lru_mm, lru_sig, lru_exp, lru_b2, lru_sqrt, lru_ix, lru_done, cl_ready = (
            sem("lru_mm"), sem("lru_sig"), sem("lru_exp"), sem("lru_b2"), sem("lru_sqrt"), sem("lru_ix"),
            sem("lru_done"), sem("cl_ready"))
        lru_cb, gated = sem("lru_cb"), sem("gated")
        z_mm, z_min, z_abs, z_ln, cum_done, eq_act, eq_dve, q_done = (
            sem("z_mm"), sem("z_min"), sem("z_abs"), sem("z_ln"), sem("cum_done"), sem("eq_act"),
            sem("eq_dve"), sem("q_done"))
        ke_turned, ke_ready, kv_mm, s_ready, s_zero, gmask_ready = (
            sem("ke_turned"), sem("ke_ready"), sem("kv_mm"), sem("s_ready"), sem("s_zero"), sem("gmask_ready"))
        sc_mm, sc_ready, o_mm, o_ready, sq_ready, rms_mm, rms_act, gla_done = (
            sem("sc_mm"), sem("sc_ready"), sem("o_mm"), sem("o_ready"), sem("sq_ready"), sem("rms_mm"),
            sem("rms_act"), sem("gla_done"))
        d_wout, d_ln1 = sem("d_wout"), sem("d_ln1")
        d_xres = [sem("d_xres0"), sem("d_xres1")]
        out_mm, y_gated, x1_ready, h2_ready, h2_stored, h2_turned, h2T_ready, logit_mm = (
            sem("out_mm"), sem("y_gated"), sem("x1_ready"), sem("h2_ready"), [sem("h2_stored0"), sem("h2_stored1")],
            sem("h2_turned"), sem("h2T_ready"), sem("logit_mm"))
        d_rt, bias_turned, bias_ready, sel_ready, rank_mm, dest_ready, wd_ready, wd_turned, wdT_ready, bd_mm, bd_used = (
            sem("d_rt"), sem("bias_turned"), sem("bias_ready"), sem("sel_ready"), sem("rank_mm"),
            sem("dest_ready"), sem("wd_ready"), sem("wd_turned"), sem("wdT_ready"), sem("bd_mm"), sem("bd_used"))
        iota_ready, top_exp_in, top_exp, tab_stored, tab_ready, rt_zeroed, rt_scattered = (
            sem("iota_ready"), sem("top_exp_in"), sem("top_exp"), sem("tab_stored"), sem("tab_ready"),
            sem("rt_zeroed"), sem("rt_scattered"))
        d_rowslot = sem("d_rowslot")
        tab_col, d_bdn, moe_clear = sem("tab_col"), sem("d_bdn"), sem("moe_clear")
        d_w = [sem(f"d_w{q}") for q in range(PIECES)]
        w_used, d_idx, xg_ready = sem("w_used"), sem("d_idx"), sem("xg_ready")
        mx_turned, xT_ready = ([sem(f"{n}{b}") for b in range(2)] for n in ("mx_turned", "xT_ready"))
        gate_mm, up_mm = sem("gate_mm"), sem("up_mm")
        bias_now = sem("bias_now")
        g_ready, sg_ready, gs_ready, t_ready, act_ready = (
            sem("g_ready"), sem("sg_ready"), sem("gs_ready"), sem("t_ready"), sem("act_ready"))
        y_act, y_dve = ([sem(f"{n}{b}") for b in range(2)] for n in ("y_act", "y_dve"))
        y_stored, yb_free = sem("y_stored"), sem("yb_free")
        d_yr = [sem("d_yr0"), sem("d_yr1")]
        gidx_ready, sidx_ready = sem("gidx_ready"), sem("sidx_ready")
        yr_used, d_ln2, fin_ready = sem("yr_used"), sem("d_ln2"), sem("fin_ready")
        fin_stored = [sem("fin_stored0"), sem("fin_stored1")]
        y0_scaled, xn_in, xn_ready = sem("y0_scaled"), sem("xn_in"), sem("xn_ready")

        JB = 5
        CQ, CK, CV = 2 * D_LRU, 2 * D_LRU + PAIRS * P, 2 * D_LRU + 2 * PAIRS * P
        CG = CV + HEADS * DV
        CA = CG + HEADS * DV
        jobs = [("v", T, None, None) for T in range(NT + NTC)]
        tiles = [("conv", j, j * P, P) for j in range(JL)]
        tiles += [("k", j, CK + j * P, P) for j in range(PAIRS)]
        tiles += [("alow", 0, CA, RANK)]
        tiles += [("q", j, CQ + j * P, P) for j in range(PAIRS)]
        tiles += [("g", j, CG + j * P, P) for j in range(HEADS)]
        tiles += [("gate", j, D_LRU + j * P, P) for j in range(JL)]
        for n, (kind, j, c0, w) in enumerate(tiles):
            for s in (segs_all if kind in ("conv", "k", "alow") else segs_lat):
                jobs.append((kind, j, s, n))
        by_act = [k in ("gate", "g") or (k == "v" and j % 2 == 0) for k, j, _, _ in jobs]
        counts, freed = [0, 0], []
        for a in by_act:
            counts[0 if a else 1] += 1
            freed.append((0 if a else 1, counts[0 if a else 1]))
        NPA, NPV = counts
        job_of = {(k, j, s): i for i, (k, j, s, _) in enumerate(jobs)}
        plan, at_job = [("job", i) for i in range(NT + NTC + 3)], NT + NTC + 3
        for lstep in range(2 * JL):
            plan += [("gate_r", lstep), ("job", at_job), ("gate_i", lstep), ("decay", lstep), ("job", at_job + 1),
                     ("job", at_job + 2), ("scan", lstep)]
            at_job += 3
        plan += [("job", i) for i in range(at_job, len(jobs))]
        last_tile = {n: i for i, (_, _, _, n) in enumerate(jobs)}
        NCONV = 3 * JL

        def arena_rev(ap, n):
            return ap[:, n - 1::-1]

        def uT_in(n):
            v = ps[4 + n % 4]
            return v[:, :].rearrange("p (r w) -> p r w", w=GRID_W) if n < 16 else v[:, 0:CTX]

        def uT_out(n):
            return colmajor(uT[:, n % 8, 0:SEQ], 8 * (n // 8), 8) if n < 16 else uT[:, n % 8, SEQ:L]

        def grid_half(ap, seg):
            w0, w1 = seg[0] // ROWS, seg[1] // ROWS
            return ap.rearrange("p (r w) -> p w r", w=GRID_W)[:, w0:w1, :]

        def half(ap):
            return ap[:, :].rearrange("p (w r) -> p w r", r=ROWS)

        def colmajor(ap, r0, nr):
            return ap.rearrange("p (w r) -> p r w", r=ROWS)[:, r0:r0 + nr, :]

        order = [[NCH + i for i in range(NCHC)] + list(range(NCH)),
                 [NCH + NCHC - 1 - i for i in range(NCHC)] + list(range(NCH))[::-1]]

        def slot(n):
            return n % 2 if n < NCHC else 2 + n - NCHC

        NS = NCHC + NCH

        def settle(eng):
            eng.sem_inc(settled[eng.engine], 1)

        block = ctxs.enter_context(nc.Block())

        @block.sync
        def _(sp):
            def rows(src, n):
                return src.rearrange("(a b) -> a b", b=P) if n else src

            at = [0]

            def param(ap, n):
                sp.dma_start(prow[at[0]:at[0] + n, :], ap).then_inc(d_par, 16)
                at[0] += n

            param(c[0].rearrange("(a b) -> a b", b=P), 8)
            param(c_ctx.rearrange("(a b) -> a b", b=P), 8)
            param(b_ada[0, 0:2 * D].rearrange("(a b) -> a b", b=P), 16)
            param(conv_w[0].rearrange("t (a b) -> (t a) b", b=P), 16)
            param(conv_b[0].rearrange("(a b) -> a b", b=P), 4)
            for v in (lru_ba, lru_bx, lru_lam):
                param(v[0].rearrange("d (a b) -> (d a) b", b=P), 8)
            param(gla_ba[0].rearrange("d (a b) -> (d a) b", b=P), 4)
            param(gla_norm_g[0].rearrange("(a b) -> a b", b=P), 4)
            wada_v = w_ada[0].rearrange("(k p) n -> p k n", p=P)

            def ada_piece(j):
                if j >= 3:
                    sp.wait_ge(ada_used, j - 2)
                sp.dma_start(wada_ring[:, j % 3], wada_v[:, :, j * 512:(j + 1) * 512]).then_inc(d_wada[j % 3], 16)

            for j in range(4):
                ada_piece(j)
            x_v = x[0].rearrange("(t p) d -> p t d", p=P)
            sp.dma_start(xin[:, 0:4], x_v[:, 0:4]).then_inc(d_x[0], 16)
            sp.dma_start(xin[:, 4:8], x_v[:, 4:8]).then_inc(d_x[1], 16)
            sp.dma_start(xin[:, 8:10], ctx[0].rearrange("(t p) d -> p t d", p=P)).then_inc(d_x[2], 16)
            sp.dma_start(adarow[:, :, :].rearrange("p a b -> p (a b)"),
                         b_ada[0:1, 2 * D:6 * D].partition_broadcast(P).rearrange("p a n -> p (a n)")).then_inc(d_bada, 16)
            for j in range(4, 12):
                ada_piece(j)
            sp.wait_ge(const_ready, 2)
            for d in range(2):
                for g, w in ((0, lru_wa), (1, lru_wx)):
                    for h in range(2):
                        q = (d * 2 + g) * JL
                        sp.dma_start(lruw[64 * h:64 * h + 64, q:q + JL, 64 * h:64 * h + 64],
                                     w[0, d].rearrange("(j h) c e -> h c j e", h=2)[h]).then_inc(d_lruw, 16)
            win_v = w_in[0].rearrange("(k p) n -> p k n", p=P)
            sp.dma_start(wv, win_v[:, :, CV:CV + 512]).then_inc(d_wv, 16)
            for n, (kind, j, c0, w) in enumerate(tiles):
                if n >= WRING:
                    sp.wait_ge(proj_done, last_tile[n - WRING] + 1)
                sp.dma_start(wring[n % WRING][:, :, 0:w], win_v[:, :, c0:c0 + w]).then_inc(d_win[n % WRING], 16)
            sp.wait_ge(lru_done, 2 * JL)
            sp.dma_start(wa_sb, gla_wa[0].rearrange("d r n -> r d n")).then_inc(d_small, 16)
            sp.wait_ge(gla_done, 4)
            sp.dma_start(wout, w_out[0].rearrange("(k p) n -> p k n", p=P)).then_inc(d_wout, 16)
            for i, v in enumerate((ln1_g, ln1_b)):
                sp.dma_start(ln1r[:, i], v.partition_broadcast(P).rearrange("p a n -> p (a n)")).then_inc(d_ln1, 16)
            sp.dma_start(wrt, w_router[0].rearrange("(k p) e -> p k e", p=P)).then_inc(d_rt, 16)
            sp.dma_start(brt, b_router.partition_broadcast(P).rearrange("p a n -> p (a n)")).then_inc(d_rt, 16)
            sp.dma_start(brow[0:NE, 0], b_gate[0]).then_inc(d_rt, 16)
            sp.dma_start(brow[0:NE, 1], b_up[0]).then_inc(d_rt, 16)
            for t in range(NT + 1):
                if t < NT:
                    if t >= 2:
                        sp.wait_ge(x1_ready, t - 1)
                    sp.dma_start(xres[:, t % 2], x[0, t * P:(t + 1) * P, :]).then_inc(d_xres[t % 2], 16)
                if t >= 1:
                    sp.wait_ge(h2_ready, t)
                    sp.dma_start(h2_dram[(t - 1) * P:t * P, :], h2b[:, (t - 1) % 2]).then_inc(h2_stored[(t - 1) % 2], 16)
            sp.wait_ge(x1_ready, NT)
            sp.dma_start(bdn[0:NE], b_down[0].unsqueeze(1)).then_inc(d_bdn, 16)
            sp.wait_ge(tab_col, 1)
            sp.dma_start(tab_dram, tabc).then_inc(tab_stored, 16)
            sp.wait_ge(tab_stored, 16)
            sp.dma_start(tab[0:1, :], tab_dram.rearrange("a b -> (a b)").unsqueeze(0)).then_inc(tab_ready, 16)
            sp.wait_ge(tab_ready, 16)
            def weights(q):
                return (w_gate, w_up, w_down)[q // 4][0].rearrange("e (q c p) n -> e q p c n", c=2, p=P)[:, q % 4]

            def piece(q, e):
                sp.dma_start(ring[q], weights(q)[ds(e, 1)].rearrange("a p c n -> p (a c) n")).then_inc(d_w[q], 16)

            e0 = sp.value_load(tab[0:1, 1:2], min_val=0, max_val=NE - 1)
            for q in range(PIECES):
                piece(q, e0)
            sp.wait_ge(rt_scattered, 16 * TOPK * NT)
            sp.dma_start(rowslot, rowslot_dram.rearrange("(b p) a -> p (b a)", p=P),
                         allow_slow_non_contiguous=True).then_inc(d_rowslot, 16)
            with sp.Fori(0, MAXU - 1) as u:
                cls = sp.value_load(tab[0:1, ds(u * 4 + 4, 1)], min_val=0, max_val=NCLS)
                with sp.If(cls > 0):
                    e = sp.value_load(tab[0:1, ds(u * 4 + 5, 1)], min_val=0, max_val=NE - 1)
                    for q in range(PIECES):
                        sp.wait_ge(w_used, PIECES * u + q + 1)
                        piece(q, e)
            nunits = sp.value_load(tab[0:1, 3:4], min_val=1, max_val=MAXU)
            sp.wait_ge(w_used, nunits * PIECES)
            for i, v in enumerate((ln2_g, ln2_b)):
                sp.dma_start(ln2r[:, i], v.partition_broadcast(P).rearrange("p a n -> p (a n)")).then_inc(d_ln2, 16)
            sp.wait_ge(y_stored, nunits * 32)
            for t in range(NT):
                if t >= 1:
                    sp.wait_ge(yr_used, t)
                for T in ((0, 1) if t == 0 else (t + 1,)):
                    if T < NT:
                        sp.dma_start(yrows[T % 2], y_dram.rearrange("(k t p) n -> t p k n", k=TOPK, p=P)[T]).then_inc(d_yr[T % 2], 16)
                sp.wait_ge(fin_ready, t + 1)
                sp.dma_start(out[0, t * P:(t + 1) * P, :], fin[:, t % 2]).then_inc(fin_stored[t % 2], 16)
            sp.wait_ge(fin_stored[0], 16 * (NT // 2))
            sp.wait_ge(fin_stored[1], 16 * (NT // 2))

        def turn_tokens(pe, b):
            for k in range(KD):
                mm = pe.transpose(ps[2 * b + k // 4][:, (k % 4) * P:(k % 4 + 1) * P], xg[:, b, k * P:(k + 1) * P],
                                  ident[:, :])
            mm.then_inc(mx_turned[b], 1)

        def expert_unit(pe, u, v, ncls):
            n, nb = STEP * v, (STEP * v + P - 1) // P
            for b in range(2):
                pe.wait_ge(xT_ready[b], u + 1)
            for g in range(2):
                if g:
                    for b in range(2):
                        pe.wait_ge(y_act[b], u + 1)
                        pe.wait_ge(y_dve[b], u + 1)
                for q in range(4):
                    pe.wait_ge(d_w[4 * g + q], 16 * u + 16)
                    for k in (2 * q, 2 * q + 1):
                        for m in range(KD):
                            mm = pe.matmul(ps[4 * g + m // 2][:, (m % 2) * WU:(m % 2) * WU + n],
                                           ring[4 * g + q][:, k % 2, m * P:(m + 1) * P], xT[:, k, 0:n],
                                           start=(k == 0 and m % 2 == 0), stop=(k == KD - 1), skip_group_check=True)
                            if k == KD - 1 and m in (1, 3, 5):
                                mm.then_inc((gate_mm, up_mm)[g], 1)
                    mm.then_inc(w_used, 1)
            pe.wait_ge(g_ready, 8 * u + 8)
            with pe.If(ncls > 0):
                pe.wait_ge(xg_ready, 32 * u + 64)
                turn_tokens(pe, 0)
                with pe.If(ncls > P // STEP):
                    turn_tokens(pe, 1)
                with pe.If(ncls <= P // STEP):
                    pe.nop().then_inc(mx_turned[1], 1)
                pe.nop()
            pe.wait_ge(t_ready, 8 * u + 8)
            for q in range(4):
                pe.wait_ge(d_w[8 + q], 16 * u + 16)
                for k in (2 * q, 2 * q + 1):
                    pe.wait_ge(act_ready, 8 * u + k + 1)
                    for b in range(nb):
                        for s in range(2):
                            mm = pe.matmul(ps[4 + 2 * b + s][:, :], act_[:, k, b * P:(b + 1) * P],
                                           ring[8 + q][:, k % 2, s * BANK:(s + 1) * BANK],
                                           start=(k == 0), stop=(k == KD - 1))
                mm.then_inc(w_used, 1)

        @block.tensor
        def _(pe):
            pe.wait_ge(const_ready, 1)
            pe.wait_ge(d_par, 16 * 10)
            pe.transpose(ps[0][:, 0:NPAR], prow[0:NPAR, :], ident[0:NPAR, 0:NPAR]).then_inc(par_turned, 1)
            pe.wait_ge(cs_ready, 1)
            for j in range(4):
                pe.wait_ge(d_wada[j % 3], 16 * (j // 3 + 1))
                for m in range(4):
                    q = 4 * j + m
                    for k in range(KD):
                        mm = pe.matmul(ps[1][:, 2 * q:2 * q + 2], wada_ring[:, j % 3, k, m * P:(m + 1) * P],
                                       csil[:, k, :], start=(k == 0), stop=(k == KD - 1))
                mm.then_inc(ada_used, 1)
            n = 0
            for grp, (t0, t1) in enumerate(((0, 4), (4, 8), (8, 10))):
                pe.wait_ge(d_x[grp], 16)
                for k in range(KD):
                    if n >= 4:
                        pe.wait_ge((uT_act, uT_dve)[n % 2], (n - 4) // 2 + 1)
                    for i, t in enumerate(range(t0, t1)):
                        mm = pe.transpose(ps[4 + n % 4][:, i * P:(i + 1) * P], xin[:, t, k * P:(k + 1) * P], ident[:, :])
                    mm.then_inc(x_turned, 1)
                    n += 1
            pe.wait_ge(csb_ready, 1)
            for j in range(4, 12):
                pe.wait_ge(d_wada[j % 3], 16 * (j // 3 + 1))
                if j >= 6:
                    pe.wait_ge(adarow_done, j - 5)
                for k in range(KD):
                    mm = pe.matmul(ps[2 + j % 2][:, :], csb[:, k, :], wada_ring[:, j % 3, k, :],
                                   start=(k == 0), stop=(k == KD - 1))
                mm.then_inc(ada_used, 1)
            pe.wait_ge(uT_act, 12)
            pe.wait_ge(uT_dve, 12)
            pe.wait_ge(adarow_done, 8)
            pe.wait_ge(d_wv, 16)

            def moving(kind, k, seg):
                if kind == "conv" and seg[0] < SEQ:
                    return colmajor(uT[:, k, 0:SEQ], seg[0] // GRID_W, 8)
                return uT[:, k, seg[0]:seg[1]]

            pe.wait_ge(d_lruw, 16 * 8)
            for what, i in plan:
                if what in ("gate_r", "gate_i"):
                    g, (j, d) = what == "gate_i", (i // 2, i % 2)
                    e, cnt = freed[job_of["conv", j, segs_all[2]]]
                    pe.wait_ge((proj_act, proj_dve)[e], cnt)
                    for b, (s0, s1) in enumerate(segs_all):
                        if 2 * i + g:
                            pe.wait_ge(lru_sig, 3 * (2 * i + g - 1) + b + 1)
                        pe.matmul(ps[JB + b][:, 0:s1 - s0], lruw[:, (d * 2 + g) * JL + j, :], XL[:, j, s0:s1],
                                  start=True, stop=True).then_inc(lru_mm, 1)
                if what != "job":
                    continue
                kind, j, seg, n = jobs[i]
                if i >= JB:
                    e, cnt = freed[i - JB]
                    pe.wait_ge((proj_act, proj_dve)[e], cnt)
                if kind == "v":
                    for k in range(KD):
                        mm = pe.matmul(ps[i % JB][:, :], uT[:, k, j * P:(j + 1) * P], wv[:, k, :], start=(k == 0), stop=(k == KD - 1))
                else:
                    w = tiles[n][3]
                    if jobs[i - 1][3] != n:
                        pe.wait_ge(d_win[n % WRING], 16 * (n // WRING + 1))
                    for k in range(KD):
                        mm = pe.matmul(ps[i % JB][0:w, 0:seg[1] - seg[0]], wring[n % WRING][:, k, 0:w],
                                       moving(kind, k, seg), start=(k == 0), stop=(k == KD - 1))
                mm.then_inc(proj_done, 1)
            pe.wait_ge(proj_dve, NPV)
            pe.wait_ge(proj_act, NPA)
            pe.wait_ge(lru_sig, 12 * JL)
            pe.wait_ge(d_small, 16)
            nz = 0
            for pr in range(PAIRS):
                if pr:
                    pe.wait_ge(rms_act, 4 * pr)
                    pe.wait_ge(o_ready, NT * pr)
                for d in range(2):
                    for s0, s1 in segs_all:
                        if d:
                            pe.wait_ge(z_min, 6 * pr + nz % 6 - 2)
                            pe.wait_ge(z_abs, 6 * pr + nz % 6 - 2)
                        pe.matmul(ps[nz % 3][:, 0:s1 - s0], wa_sb[:, d, pr * P:(pr + 1) * P], AL[0:RANK, s0:s1],
                                  start=True, stop=True).then_inc(z_mm, 1)
                        nz += 1
                pe.wait_ge(z_min, 6 * pr + 6)
                pe.wait_ge(z_abs, 6 * pr + 6)
                for d in range(2):
                    pe.wait_ge(q_done, 2 * pr + d + 1)
                    for b, (t0, t1) in enumerate(((0, 4), (4, 8), (8, 10))):
                        for t in range(t0, t1):
                            mm = pe.transpose(ps[3 * d + b][:, (t - t0) * P:(t - t0 + 1) * P],
                                              gKE[:, d, t * P:(t + 1) * P], ident[:, :])
                        mm.then_inc(ke_turned, 1)
                pe.wait_ge(ke_ready, 6 * (pr + 1))
                for n in range(NS - 1):
                    for d in range(2):
                        ch = order[d][n]
                        T, h = ch // 2, ch % 2
                        if n >= 4:
                            pe.wait_ge(s_ready, 2 * (pr * 2 * (NS - 1) + 2 * (n - 4) + d + 1))
                        pe.matmul(ps[4 * d + n % 4][:, 0:2 * DV], gKT[64 * h:64 * h + 64, d, T, :],
                                  V[64 * h:64 * h + 64, T, 2 * pr * DV:(2 * pr + 2) * DV],
                                  start=True, stop=True).then_inc(kv_mm, 1)
                pe.wait_ge(s_ready, 4 * (pr + 1) * (NS - 1))

                def scores(T):
                    if T >= 2:
                        pe.wait_ge(sc_ready, 4 * (NT * pr + T - 1))
                    for d in range(2):
                        for h in range(2):
                            mm = pe.matmul(ps[2 * (T % 2) + h][:, d * P:(d + 1) * P],
                                           gK[64 * h:64 * h + 64, d, T * P:(T + 1) * P],
                                           gQ[64 * h:64 * h + 64, d, T * P:(T + 1) * P], start=True, stop=True)
                            mm.then_inc(sc_mm, 1)

                scores(0)
                for T in range(NT):
                    if T + 1 < NT:
                        scores(T + 1)
                    pe.wait_ge(sc_ready, 4 * (NT * pr + T + 1))
                    if T >= 2:
                        pe.wait_ge(o_ready, NT * pr + T - 1)
                    for h in range(2):
                        o_ = ps[4 + T % 2][:, h * P:(h + 1) * P]
                        vh = V[:, T, (2 * pr + h) * DV:(2 * pr + h + 1) * DV]
                        pe.matmul(o_, vh, gSc[:, T % 2, h, 0, :], start=True, stop=False, skip_group_check=True)
                        pe.matmul(o_, vh, gSc[:, T % 2, h, 1, :], start=False, stop=False, skip_group_check=True)
                        for cc in range(2):
                            for d in range(2):
                                ch = 2 * T + cc
                                mm = pe.matmul(o_[:, cc * CH:(cc + 1) * CH], gS[:, d, slot(order[d].index(ch)), h, :],
                                               gQ[:, d, ch * CH:(ch + 1) * CH], start=False,
                                               stop=(cc == 1 and d == 1), skip_group_check=True)
                    mm.then_inc(o_mm, 1)
                for h in range(2):
                    pe.wait_ge(sq_ready, 2 * pr + h + 1)
                    for s in range(2):
                        pe.matmul(ps[6 + s][:, :], ones[:, :], gSq[:, h, s * BANK:(s + 1) * BANK],
                                  start=True, stop=True).then_inc(rms_mm, 1)
                    if h == 0:
                        pe.wait_ge(rms_act, 4 * pr + 2)
            pe.wait_ge(gla_done, 4)
            pe.wait_ge(rms_act, 8)
            pe.wait_ge(gated, 2 * JL)
            pe.wait_ge(d_wout, 16)
            pe.wait_ge(d_rt, 64)
            for t in range(NT + 1):
                if t < NT:
                    if t >= 2:
                        pe.wait_ge(y_gated, 2 * (t - 1))
                    for s in range(2):
                        for k in range(KD):
                            mm = pe.matmul(ps[2 * (t % 2) + s][:, :], YT[:, k, t * P:(t + 1) * P],
                                           wout[:, k, s * BANK:(s + 1) * BANK], start=(k == 0), stop=(k == KD - 1))
                        mm.then_inc(out_mm, 1)
                if t >= 1:
                    T = t - 1
                    pe.wait_ge(h2_ready, T + 1)
                    if T >= 1:
                        pe.wait_ge(h2T_ready, 2 * T)
                    for k in range(KD):
                        mm = pe.transpose(ps[4 + k // 4][:, (k % 4) * P:(k % 4 + 1) * P],
                                          h2b[:, T % 2, k * P:(k + 1) * P], ident[:, :])
                        if k % 4 == 3:
                            mm.then_inc(h2_turned, 1)
                    pe.wait_ge(h2T_ready, 2 * T + 2)
                    for k in range(KD):
                        mm = pe.matmul(ps[6][:, T * NE:(T + 1) * NE], h2T[:, k, :], wrt[:, k, :],
                                       start=(k == 0), stop=(k == KD - 1))
                    mm.then_inc(logit_mm, 1)
            for g in range(2):
                for k in range(KD):
                    mm = pe.transpose(ps[7][:, (g * KD + k) * NE:(g * KD + k + 1) * NE],
                                      brow[0:NE, g, k * P:(k + 1) * P], ident[0:NE, 0:NE])
            mm.then_inc(bias_turned, 1)
            pe.wait_ge(sel_ready, 1)
            for T in range(NT):
                for s in range(T):
                    pe.matmul(ps[0][:, T * NE:(T + 1) * NE], ones[:, :], Mx[:, s, :], start=(s == 0), stop=False)
                pe.matmul(ps[0][:, T * NE:(T + 1) * NE], tri[:, :], Mx[:, T, :], start=(T == 0), stop=True)
            for T in range(NT):
                mm = pe.matmul(ps[1][:, 0:NE], ones[:, :], Mx[:, T, :], start=(T == 0), stop=(T == NT - 1))
            mm.then_inc(rank_mm, 1)
            pe.wait_ge(d_bdn, 16)
            pe.wait_ge(wd_ready, 1)
            for T in range(NT):
                if T:
                    pe.wait_ge(wdT_ready, T)
                pe.transpose(ps[6][0:NE, 0:P], Wd[:, T, :], ident[:, :]).then_inc(wd_turned, 1)
                pe.wait_ge(wdT_ready, T + 1)
                if T:
                    pe.wait_ge(bd_used, 2 * T)
                for s in range(2):
                    pe.matmul(ps[2 + s][:, :], WdT[0:NE, :], bdn[0:NE, 0, s * BANK:(s + 1) * BANK],
                              start=True, stop=True).then_inc(bd_mm, 1)
            pe.wait_ge(bias_ready, 1)
            pe.wait_ge(dest_ready, 1)
            pe.wait_ge(bd_used, 2 * NT)
            pe.wait_ge(tab_ready, 16)
            cls0 = pe.value_load(tab[0:1, 0:1], min_val=0, max_val=NCLS)
            pe.wait_ge(xg_ready, 32)
            turn_tokens(pe, 0)
            with pe.If(cls0 > P // STEP):
                turn_tokens(pe, 1)
            with pe.If(cls0 <= P // STEP):
                pe.nop().then_inc(mx_turned[1], 1)
            with pe.Fori(0, MAXU) as u:
                cls = pe.value_load(tab[0:1, ds(u * 4, 1)], min_val=0, max_val=NCLS)
                with pe.If(cls > 0):
                    ncls = pe.value_load(tab[0:1, ds(u * 4 + 4, 1)], min_val=0, max_val=NCLS)
                    for v in CLASSES:
                        with pe.If(cls == v):
                            expert_unit(pe, u, v, ncls)
                        pe.nop()

        @block.scalar
        def _(act):
            ch = Chain(act, ach)
            act.wait_ge(par_ready, 1)
            act.activation(csil[:, :, :], par[:, 0:2 * KD].rearrange("p (a k) -> p k a", a=2), ACT.Silu).then_inc(cs_ready, 1)
            act.wait_ge(par_ready, 2)
            act.activation(small[:, 0:8], small[:, 0:8], ACT.Exp, scale=-1.0).then_inc(cs_ready, 1)
            act.wait_ge(ada1_ready, 1)
            for n in range(0, 24, 2):
                grp, k = n // 8, n % 8
                w, c0, who = (512, 512 * grp, 0) if grp < 2 else (256, 1024, 1)
                act.wait_ge(x_turned, n + 1)
                act.activation(uT_out(n), uT_in(n), ACT.Identity,
                               bias=ada1[:, 0, k, who:who + 1], scale=ada1[:, 1, k, who:who + 1]).then_inc(uT_act, 1)
            act.wait_ge(cl_ready, 2)
            for what, i in plan:
                if what in ("gate_r", "gate_i"):
                    g, (j, d) = what == "gate_i", (i // 2, i % 2)
                    if i and not g:
                        act.wait_ge(lru_cb, i)
                    elif i:
                        act.wait_ge(lru_done, i)
                    if i == 0 and not g:
                        act.wait_ge(proj_done, NT + NTC)
                    for b, (s0, s1) in enumerate(segs_all):
                        act.wait_ge(lru_mm, 3 * (2 * i + g) + b + 1)
                        act.activation((lB, lC)[g][:, s0:s1], ps[JB + b][:, 0:s1 - s0], ACT.Sigmoid,
                                       bias=par[:, (C_BA, C_BX)[g] + d * JL + j:(C_BA, C_BX)[g] + d * JL + j + 1]).then_inc(lru_sig, 1)
                elif what == "decay":
                    j, d = i // 2, i % 2
                    act.wait_ge(lru_sig, 6 * i + 6)
                    act.activation(lA, lB, ACT.Exp, scale=cl[:, d * JL + j:d * JL + j + 1]).then_inc(lru_exp, 1)
                    act.wait_ge(lru_exp, 2 * i + 1)
                    act.activation(lB, lB, ACT.Tanh, scale=ncl[:, d * JL + j:d * JL + j + 1]).then_inc(lru_exp, 1)
                elif what == "scan":
                    act.wait_ge(lru_b2, i + 1)
                    act.activation(lB, lB, ACT.Sqrt).then_inc(lru_sqrt, 1)
                else:
                    kind, j, seg, n = jobs[i]
                    src = ps[i % JB]
                    if kind == "conv":
                        act.wait_ge(proj_done, i + 1)
                        act.activation(XL[:, j, seg[0]:seg[1]], src[:, 0:seg[1] - seg[0]], ACT.Identity,
                                       bias=par[:, C_CONVB + j:C_CONVB + j + 1],
                                       scale=par[:, C_CONVW + 2 * JL + j:C_CONVW + 2 * JL + j + 1]).then_inc(conv_started, 1)
                    elif by_act[i]:
                        act.wait_ge(proj_done, i + 1)
                        if kind == "v":
                            act.copy(V[:, j, :], src[:, :]).then_inc(proj_act, 1)
                        elif kind == "gate":
                            if seg == segs_lat[0] and j == 0:
                                act.wait_ge(lru_done, 2 * JL)
                            act.activation(gelu_[:, 2 * j + seg[0] // BANK], src[:, :], ACT.Gelu_apprx_tanh).then_inc(proj_act, 1)
                        else:
                            act.activation(grid_half(YT[:, JL + j], seg), half(src), ACT.Silu).then_inc(proj_act, 1)
            nz = 0
            act.wait_ge(gmask_ready, 2)
            for pr in range(PAIRS):
                for d in range(2):
                    if pr + d:
                        act.wait_ge(q_done, 2 * pr + d)
                    gbias = par[:, C_GBA + d * PAIRS + pr:C_GBA + d * PAIRS + pr + 1]
                    for s0, s1 in segs_all:
                        act.wait_ge(z_mm, nz + 1)
                        act.activation(gE[:, s0:s1], ps[nz % 3][:, 0:s1 - s0], ACT.Abs, bias=gbias).then_inc(z_abs, 1)
                        nz += 1
                    act.wait_ge(z_abs, nz)
                    ch.link(act.activation(gE, gE, ACT.Exp, scale=-1.0))
                    act.activation(gE, gE, ACT.Ln, bias=1.0).then_inc(z_ln, 1)
                    act.wait_ge(cum_done, 3 * (2 * pr + d) + 1)
                    for m, sc in ((0, 1.0), (1, -1.0)):
                        if m:
                            act.wait_ge(eq_dve, 2 * (2 * pr + d) + 1)
                        act.activation(gE[:, 0:SEQ], gBC[:, d, 0:SEQ], ACT.Exp, scale=sc / 16).then_inc(eq_act, 1)
                    act.wait_ge(cum_done, 3 * (2 * pr + d) + 3)
                    act.activation(gKE[:, d], gKE[:, d], ACT.Exp, scale=1.0 / 16).then_inc(eq_act, 1)
                    act.activation(small[:, 0:NS] if d == 0 else small[:, 20:20 + NS],
                                   small[:, 0:NS] if d == 0 else small[:, 20:20 + NS], ACT.Exp,
                                   scale=1.0 / 16).then_inc(eq_act, 1)
                for b in range(6):
                    act.wait_ge(ke_turned, 6 * pr + b + 1)
                    w = 512 if b % 3 < 2 else 256
                    act.copy(gKT[:, b // 3, 4 * (b % 3):4 * (b % 3) + w // P, :],
                             ps[b][:, 0:w].rearrange("p (a b) -> p a b", b=P)).then_inc(ke_ready, 1)
                for T in range(NT):
                    act.wait_ge(o_mm, NT * pr + T + 1)
                    act.copy(gO[:, :, T * P:(T + 1) * P],
                             ps[4 + T % 2][:, 0:2 * P].rearrange("p (h b) -> p h b", h=2)).then_inc(o_ready, 1)
                act.wait_ge(o_ready, NT * (pr + 1))
                for h in range(2):
                    act.activation(gSq[:, h], gO[:, h], ACT.Square).then_inc(sq_ready, 1)
                for h in range(2):
                    for s in range(2):
                        act.wait_ge(rms_mm, 4 * pr + 2 * h + s + 1)
                        act.activation(gSq[:, h, s * BANK:(s + 1) * BANK], ps[6 + s][:, :], ACT.Sqrt,
                                       scale=1.0 / DV, bias=eps_rms[:, :]).then_inc(rms_act, 1)
            def std(n):
                act.wait_ge(var_ready, n + 1)
                act.activation(small[:, 48:49], small[:, 13:14], ACT.Sqrt, bias=eps_ln[:, :]).then_inc(std_ready, 1)

            std(0)
            for T in range(NT):
                if T + 1 < NT:
                    std(T + 1)
                for b in range(2):
                    act.wait_ge(h2_turned, 2 * T + b + 1)
                    if b == 0 and T:
                        act.wait_ge(logit_mm, T)
                    act.copy(h2T[:, 4 * b:4 * b + 4, :], ps[4 + b][:, :].rearrange("p (a b) -> p a b", b=P)).then_inc(h2T_ready, 1)
            act.wait_ge(top_exp_in, 1)
            act.activation(ev, ev, ACT.Exp).then_inc(top_exp, 1)
            for T in range(NT):
                act.wait_ge(wd_turned, T + 1)
                if T == 0:
                    act.wait_ge(logit_mm, NT)
                if T:
                    act.wait_ge(bd_mm, 2 * T)
                act.copy(WdT[0:NE, :], ps[6][0:NE, 0:P]).then_inc(wdT_ready, 1)
            act.wait_ge(tab_ready, 16)
            for b in range(2):
                act.nop().then_inc(y_act[b], 1)

            def take_tokens(b, n):
                act.wait_ge(mx_turned[b], n)
                for j in range(2):
                    mm = act.copy(xT[:, 4 * j:4 * j + 4, b * P:(b + 1) * P],
                                  ps[2 * b + j][:, :].rearrange("p (k n) -> p k n", k=4))
                mm.then_inc(xT_ready[b], 1)

            cls0 = act.value_load(tab[0:1, 0:1], min_val=0, max_val=NCLS)
            take_tokens(0, 1)
            with act.If(cls0 > P // STEP):
                take_tokens(1, 1)
            with act.If(cls0 <= P // STEP):
                act.nop().then_inc(xT_ready[1], 1)
            with act.Fori(0, MAXU) as u:
                cls = act.value_load(tab[0:1, ds(u * 4, 1)], min_val=0, max_val=NCLS)
                with act.If(cls > 0):
                    ncls = act.value_load(tab[0:1, ds(u * 4 + 4, 1)], min_val=0, max_val=NCLS)
                    for v in CLASSES:
                        with act.If(cls == v):
                            n = STEP * v
                            for m in range(0, KD, 2):
                                act.wait_ge(g_ready, 8 * u + m + 2)
                                act.activation(sg[:, m:m + 2, 0:n], gb[:, m:m + 2, 0:n], ACT.Sigmoid,
                                               scale=SWIGLU).then_inc(sg_ready, 1)
                    with act.If(ncls > 0):
                        take_tokens(0, u + 2)
                        with act.If(ncls > P // STEP):
                            take_tokens(1, u + 2)
                        with act.If(ncls <= P // STEP):
                            act.nop().then_inc(xT_ready[1], 1)
                        act.nop()
                    act.wait_ge(yb_free, u + 1)
                    act.wait_ge(w_used, PIECES * u + PIECES)
                    act.copy(yb[:, 0, 0:BANK], ps[4][:, :]).then_inc(y_act[0], 1)
                    with act.If(cls > P // STEP):
                        act.copy(yb[:, 1, 0:BANK], ps[6][:, :]).then_inc(y_act[1], 1)
                    with act.If(cls <= P // STEP):
                        act.nop().then_inc(y_act[1], 1)
                    act.nop()
            for T in range(NT):
                act.wait_ge(d_yr[T % 2], 16 * (T // 2 + 1))
                act.activation(acc[:, T % 2], yrows[T % 2][:, 0], ACT.Copy, scale=topw[:, T, 0:1]).then_inc(y0_scaled, 1)
                std(NT + T)
                act.wait_ge(xn_in, T + 1)
                if T >= 2:
                    act.wait_ge(fin_stored[T % 2], 16 * (T // 2))
                act.activation(fin[:, T % 2], acc[:, T % 2], ACT.Identity, bias=small[:, 50:51],
                               scale=small[:, 49:50]).then_inc(xn_ready, 1)

        @block.vector
        def _(dve):
            ch = Chain(dve, vch)
            link = ch.link
            dve.wait_ge(par_turned, 1)
            link(dve.tensor_copy(par[:, :], ps[0][:, 0:NPAR]))
            dve.nop().then_inc(par_ready, 1)
            link(dve.tensor_scalar(small[:, 8:16], par[:, C_LAM:C_LAM + 8], -1.0, None, ALU.mult))
            link(dve.tensor_tensor(small[:, 0:8], small[:, 8:16], par[:, C_LAM:C_LAM + 8], ALU.max))
            link(dve.tensor_scalar(small[:, 8:16], small[:, 8:16], 0.0, None, ALU.max))
            dve.nop().then_inc(par_ready, 1)
            dve.wait_ge(cs_ready, 2)
            link(dve.tensor_scalar(small[:, 16:24], small[:, 0:8], 2.0, None, ALU.add))
            link(dve.reciprocal(small[:, 16:24], small[:, 16:24]))
            link(dve.tensor_tensor(small[:, 16:24], small[:, 16:24], small[:, 0:8], ALU.mult))
            link(dve.tensor_tensor(small[:, 24:32], small[:, 16:24], small[:, 16:24], ALU.mult))
            link(dve.tensor_scalar(small[:, 0:8], small[:, 24:32], 1.0 / 15, 1.0 / 13, ALU.mult, ALU.add))
            for q in (11, 9, 7, 5, 3, 1):
                link(dve.tensor_tensor(small[:, 0:8], small[:, 0:8], small[:, 24:32], ALU.mult))
                link(dve.tensor_scalar(small[:, 0:8], small[:, 0:8], 1.0 / q, None, ALU.add))
            link(dve.tensor_tensor(small[:, 0:8], small[:, 0:8], small[:, 16:24], ALU.mult))
            link(dve.scalar_tensor_tensor(out=small[:, 0:8], in0=small[:, 0:8], scalar=2.0, in1=small[:, 8:16],
                                          op0=ALU.mult, op1=ALU.add))
            dve.tensor_scalar(cl[:, :], small[:, 0:8], -8.0, None, ALU.mult).then_inc(cl_ready, 1)
            dve.tensor_scalar(ncl[:, :], small[:, 0:8], 8.0, None, ALU.mult).then_inc(cl_ready, 1)
            dve.tensor_copy(csb, csil[:, :, 0:1].to_broadcast([P, KD, P])).then_inc(csb_ready, 1)
            dve.wait_ge(ada_used, 4)
            pada = ps[1][:, 0:4 * KD].rearrange("p (s k a) -> p s k a", s=2, a=2)
            for a in range(2):
                mm = dve.tensor_tensor(ada1[:, :, :, a], pada[:, :, :, a],
                                       par[:, C_BADA:C_BADA + 2 * KD].rearrange("p (s k) -> p s k", s=2), ALU.add)
                link(mm)
            dve.tensor_scalar(ada1[:, 1], ada1[:, 1], 1.0, None, ALU.add).then_inc(ada1_ready, 1)
            dve.wait_ge(ada1_ready, 1)
            for n in range(1, 24, 2):
                grp, k = n // 8, n % 8
                w, c0, who = (512, 512 * grp, 0) if grp < 2 else (256, 1024, 1)
                dve.wait_ge(x_turned, n + 1)
                dve.tensor_scalar(uT_out(n), uT_in(n), ada1[:, 1, k, who:who + 1],
                                  ada1[:, 0, k, who:who + 1], ALU.mult, ALU.add).then_inc(uT_dve, 1)
            dve.wait_ge(d_bada, 16)
            arow = adarow[:, :, :].rearrange("p a b -> p (a b)")
            for j in range(4, 12):
                dve.wait_ge(ada_used, j + 1)
                q = slice((j - 4) * 512, (j - 3) * 512)
                dve.tensor_tensor(arow[:, q], ps[2 + j % 2][:, :], arow[:, q], ALU.add).then_inc(adarow_done, 1)
            dve.wait_ge(adarow_done, 8)
            link(dve.tensor_scalar(adarow[:, 2], adarow[:, 2], 1.0, None, ALU.add))
            nconv = 0
            for what, i in plan:
                if what == "decay":
                    dve.wait_ge(lru_exp, 2 * i + 1)
                    link(dve.tensor_tensor(lT, lA, lA, ALU.mult))
                    dve.wait_ge(lru_exp, 2 * i + 2)
                    dve.scalar_tensor_tensor(out=lB, in0=lT, scalar=1.0, in1=lB, op0=ALU.add,
                                             op1=ALU.mult).then_inc(lru_b2, 1)
                elif what == "scan":
                    j, d = i // 2, i % 2
                    dve.wait_ge(lru_ix, i + 1)
                    dve.wait_ge(lru_sqrt, i + 1)
                    dve.tensor_tensor(lC, lC, lB, ALU.mult).then_inc(lru_cb, 1)
                    dve.wait_ge(lru_cb, i + 1)
                    cs = slice(SEQ, L) if d == 0 else slice(L - 1, SEQ - 1, -1)
                    hc = lT[:, SEQ:L] if d == 0 else lT[:, L - 1:SEQ - 1:-1]
                    link(dve.tensor_tensor_scan(hc, lA[:, cs], lC[:, cs], 0.0, ALU.mult, ALU.add))
                    last = lT[:, L - 1:L] if d == 0 else lT[:, SEQ:SEQ + 1]
                    if d == 0:
                        dve.tensor_tensor_scan(lH[:, j], lA[:, 0:SEQ], lC[:, 0:SEQ], last, ALU.mult,
                                               ALU.add).then_inc(lru_done, 1)
                        dve.wait_ge(lru_done, i + 1)
                    else:
                        link(dve.tensor_tensor_scan(arena_rev(lT, SEQ), arena_rev(lA, SEQ), arena_rev(lC, SEQ), last,
                                                    ALU.mult, ALU.add))
                        dve.tensor_tensor(lH[:, j], lH[:, j], lT[:, 0:SEQ], ALU.add).then_inc(lru_done, 1)
                        dve.wait_ge(lru_done, i + 1)
                if what != "job":
                    continue
                kind, j, seg, n = jobs[i]
                src = ps[i % JB]
                if kind == "gate":
                    dve.wait_ge(proj_act, freed[i][1])
                    yh = grid_half(YT[:, j], seg)
                    dve.tensor_tensor(yh, yh, half(gelu_[:, 2 * j + seg[0] // BANK]), ALU.mult).then_inc(gated, 1)
                if by_act[i]:
                    continue
                if kind == "conv":
                    nconv += 1
                    dve.wait_ge(conv_started, nconv)
                    s0, s1 = seg
                    rw = GRID_W if s0 < SEQ else CTX
                    o3 = XL[:, j, s0:s1].rearrange("p (r w) -> p r w", w=rw)
                    i3 = src[:, 0:s1 - s0].rearrange("p (r w) -> p r w", w=rw)
                    for tap, sh in ((0, -2), (1, -1), (3, 1)):
                        a, b = max(0, -sh), rw - max(0, sh)
                        wt = par[:, C_CONVW + tap * JL + j:C_CONVW + tap * JL + j + 1]
                        mm = dve.scalar_tensor_tensor(out=o3[:, :, a:b], in0=i3[:, :, a + sh:b + sh], scalar=wt,
                                                      in1=o3[:, :, a:b], op0=ALU.mult, op1=ALU.add)
                        if tap < 3:
                            link(mm)
                    mm.then_inc(proj_dve, 1)
                    continue
                dve.wait_ge(proj_done, i + 1)
                if kind == "v":
                    dve.tensor_copy(V[:, j, :], src[:, :]).then_inc(proj_dve, 1)
                elif kind == "alow":
                    s0, s1 = seg
                    dve.tensor_copy(AL[0:RANK, s0:s1], src[0:RANK, 0:s1 - s0]).then_inc(proj_dve, 1)
                else:
                    s0, s1 = seg
                    dst, scale = (QT, DK ** -0.5) if kind == "q" else (KT, 1.0)
                    dve.tensor_scalar(dst[:, j, s0:s1], src[:, 0:s1 - s0], scale, None, ALU.mult).then_inc(proj_dve, 1)
            dve.wait_ge(const_ready, 3)
            dve.wait_ge(proj_act, NPA)
            dve.wait_ge(gated, 2 * JL)
            link(dve.memset(gS, 0.0))
            link(dve.memset(gSc, 0.0))
            for d in range(2):
                link(dve.memset(gMask[d], 1.0))
                edge = gMask[d].rearrange("p (n c) -> p n c", c=CH)[:, :, (0, CH - 1)[d]:(0, CH - 1)[d] + 1]
                link(dve.memset(edge, 0.0))
                dve.nop().then_inc(gmask_ready, 1)
            nz = 0
            ns = 0
            for pr in range(PAIRS):
                for d in range(2):
                    gbias = par[:, C_GBA + d * PAIRS + pr:C_GBA + d * PAIRS + pr + 1]
                    g = 2 * pr + d
                    if pr:
                        dve.wait_ge(gla_done, 2)
                    for s0, s1 in segs_all:
                        dve.wait_ge(z_abs, nz + 1)
                        dve.tensor_scalar(gKE[:, d, s0:s1], ps[nz % 3][:, 0:s1 - s0], gbias, 0.0, ALU.add,
                                          ALU.min).then_inc(z_min, 1)
                        nz += 1
                    dve.wait_ge(z_min, nz)
                    dve.wait_ge(z_ln, g + 1)
                    link(dve.tensor_tensor(gKE[:, d], gKE[:, d], gE, ALU.subtract))
                    if d == 0:
                        link(dve.tensor_tensor_scan(gBC[:, 0], gMask[0], gKE[:, 0], 0.0, ALU.mult, ALU.add))
                    else:
                        link(dve.tensor_tensor_scan(arena_rev(gBC[:, 1], L), arena_rev(gMask[1], L),
                                                    arena_rev(gKE[:, 1], L), 0.0, ALU.mult, ALU.add))
                    dve.nop().then_inc(cum_done, 1)
                    bc3 = gBC[:, d].rearrange("p (n c) -> p n c", c=CH)
                    btot = bc3[:, :, CH - 1:CH] if d == 0 else bc3[:, :, 0:1]
                    ke3 = gKE[:, d].rearrange("p (n c) -> p n c", c=CH)
                    dcol = small[:, 20 * d:20 * d + NS]
                    dve.tensor_copy(dcol.unsqueeze(2), btot).then_inc(cum_done, 1)
                    dve.tensor_tensor(ke3, btot.to_broadcast([P, NS, CH]), bc3, ALU.subtract).then_inc(cum_done, 1)
                    dve.wait_ge(eq_act, 4 * g + 1)
                    dve.tensor_tensor(gQ[:, d], gE[:, 0:SEQ], QT[:, pr], ALU.mult).then_inc(eq_dve, 1)
                    dve.wait_ge(eq_act, 4 * g + 2)
                    dve.tensor_tensor(gK[:, d], gE[:, 0:SEQ], KT[:, pr, 0:SEQ], ALU.mult).then_inc(eq_dve, 1)
                    dve.wait_ge(eq_dve, 2 * g + 2)
                    dve.wait_ge(eq_act, 4 * g + 4)
                    dve.tensor_tensor(gKE[:, d], gKE[:, d], KT[:, pr], ALU.mult).then_inc(q_done, 1)
                for n in range(NS - 1):
                    for d in range(2):
                        chn = order[d][n]
                        dve.wait_ge(kv_mm, pr * 2 * (NS - 1) + 2 * n + d + 1)
                        if n:
                            dve.wait_ge(s_ready, 2 * (pr * 2 * (NS - 1) + 2 * (n - 1) + d + 1))
                        for h in range(2):
                            q = slice(64 * h, 64 * h + 64)
                            pk = ps[4 * d + n % 4][q, h * DV:(h + 1) * DV]
                            if n == 0:
                                dve.tensor_copy(gS[q, d, slot(1), h, :], pk).then_inc(s_ready, 1)
                            else:
                                dve.scalar_tensor_tensor(out=gS[q, d, slot(n + 1), h, :], in0=gS[q, d, slot(n), h, :],
                                                         scalar=small[q, 20 * d + chn:20 * d + chn + 1], in1=pk,
                                                         op0=ALU.mult, op1=ALU.add).then_inc(s_ready, 1)
                for T in range(NT):
                    if T >= 2:
                        dve.wait_ge(o_mm, NT * pr + T - 1)
                    for h in range(2):
                        dve.wait_ge(sc_mm, 4 * (NT * pr + T + 1))
                        for d in range(2):
                            dve.copy_predicated(gSc[:, T % 2, h, d, :], masks[:, d, :],
                                                ps[2 * (T % 2) + h][:, d * P:(d + 1) * P]).then_inc(sc_ready, 1)
                for h in range(2):
                    H = 2 * pr + h
                    dve.wait_ge(rms_act, 4 * pr + 2 * h + 2)
                    link(dve.reciprocal(gSq[:, h], gSq[:, h]))
                    link(dve.scalar_tensor_tensor(out=gO[:, h], in0=gO[:, h], scalar=par[:, C_GN + H:C_GN + H + 1],
                                                  in1=gSq[:, h], op0=ALU.mult, op1=ALU.mult))
                    yv = YT[:, JL + H].rearrange("p (r w) -> p r w", w=GRID_W)
                    ov = gO[:, h].rearrange("p (w r) -> p r w", r=ROWS)
                    dve.tensor_tensor(yv, yv, ov, ALU.mult).then_inc(gla_done, 1)
            dve.wait_ge(gla_done, 4)
            dve.wait_ge(d_ln1, 32)
            st, mv = small[:, 0:12], small[:, 12:14]

            nstat = [0]

            def stats(v):
                for s in range(2):
                    link(dve.bn_stats(st[:, 6 * s:6 * s + 6], v[:, s * BANK:(s + 1) * BANK]))
                link(dve.bn_aggr(mv, st))
                dve.nop().then_inc(var_ready, 1)
                nstat[0] += 1
                dve.wait_ge(std_ready, nstat[0])
                link(dve.reciprocal(small[:, 49:50], small[:, 48:49]))

            for t in range(NT):
                yv = ybuf[:, t % 2]
                if t >= 2:
                    dve.wait_ge(x1_ready, t - 1)
                for s in range(2):
                    q = slice(s * BANK, (s + 1) * BANK)
                    dve.wait_ge(out_mm, 2 * t + s + 1)
                    dve.tensor_tensor(yv[:, q], ps[2 * (t % 2) + s][:, :], adarow[:, 0, q], ALU.mult).then_inc(y_gated, 1)
                dve.wait_ge(y_gated, 2 * t + 2)
                dve.wait_ge(d_xres[t % 2], 16 * (t // 2 + 1))
                link(dve.scalar_tensor_tensor(out=yv, in0=xres[:, t % 2], scalar=ALPHA, in1=yv, op0=ALU.mult, op1=ALU.add))
                stats(yv)
                link(dve.tensor_scalar(yv, yv, mv[:, 0:1], small[:, 49:50], ALU.subtract, ALU.mult))
                link(dve.tensor_tensor(yv, yv, ln1r[:, 0], ALU.mult))
                dve.tensor_tensor(X1[:, t], yv, ln1r[:, 1], ALU.add).then_inc(x1_ready, 1)
            dve.wait_ge(logit_mm, NT)
            dve.wait_ge(iota_ready, 2)
            for b in range(2):
                dve.wait_ge(h2_stored[b], 8 * NT)
            link(dve.tensor_tensor(lgt, ps[6][:, 0:NT * NE].rearrange("p (t e) -> p t e", t=NT),
                                   brt.unsqueeze(1).to_broadcast([P, NT, NE]), ALU.add))
            for T in range(NT):
                link(dve.max(mx8[:, T], lgt[:, T]))
                link(dve.max_index(ix8[:, T], mx8[:, T], lgt[:, T]))
            link(dve.tensor_copy(iot, ioti2))
            link(dve.tensor_copy(ixf, ix8))
            for k in range(TOPK):
                link(dve.tensor_tensor(OH[:, k], iot.unsqueeze(1).to_broadcast([P, NT, NE]),
                                       ixf[:, :, k:k + 1].to_broadcast([P, NT, NE]), ALU.is_equal))
            link(dve.tensor_tensor(Mx, OH[:, 0], OH[:, 1], ALU.add))
            link(dve.tensor_tensor(Mx, Mx, OH[:, 2], ALU.add))
            link(dve.tensor_tensor(Mx, Mx, OH[:, 3], ALU.add))
            dve.nop().then_inc(sel_ready, 1)
            dve.tensor_tensor(ev, mx8[:, :, 0:TOPK], mx8[:, :, 0:1].to_broadcast([P, NT, TOPK]), ALU.subtract).then_inc(top_exp_in, 1)
            dve.wait_ge(top_exp, 1)
            sm, rc = small[:, 0:8], small[:, 8:16]
            link(dve.tensor_reduce(sm, ev, AX_X, ALU.add))
            link(dve.reciprocal(rc, sm))
            link(dve.tensor_tensor(topw, ev, rc.unsqueeze(2).to_broadcast([P, NT, TOPK]), ALU.mult))
            link(dve.tensor_tensor(Wd, OH[:, 0], topw[:, :, 0:1].to_broadcast([P, NT, NE]), ALU.mult))
            for k in range(1, TOPK):
                link(dve.tensor_tensor(tmpO, OH[:, k], topw[:, :, k:k + 1].to_broadcast([P, NT, NE]), ALU.mult))
                link(dve.tensor_tensor(Wd, Wd, tmpO, ALU.add))
            dve.nop().then_inc(wd_ready, 1)
            dve.wait_ge(rank_mm, 1)
            CNT, NB, IB, BASE, NU, IU, US, ON, T0, T1 = range(10)
            r = lambda i: rt[:, i]
            ri = lambda i: rt[:, i].bitcast(I32)
            link(dve.tensor_copy(r(CNT), ps[1][:, 0:NE]))
            link(dve.memset(r(ON), 1.0))

            def blocks(dst, cum, sh):
                link(dve.tensor_scalar(ri(T0), r(CNT), float((1 << sh) - 1), None, ALU.add))
                link(dve.tensor_scalar(ri(T1), ri(T0), sh, None, ALU.logical_shift_right))
                link(dve.tensor_copy(r(dst), ri(T1)))
                link(dve.tensor_tensor_scan(r(cum), r(ON), r(dst), 0.0, ALU.mult, ALU.add))

            blocks(NB, IB, 7)
            link(dve.tensor_tensor(r(BASE), r(IB), r(NB), ALU.subtract))
            link(dve.tensor_scalar(r(BASE), r(BASE), 128.0, None, ALU.mult))
            blocks(NU, IU, 8)
            link(dve.tensor_tensor(r(US), r(IU), r(NU), ALU.subtract))
            link(dve.tensor_tensor(Gx, ps[0][:, 0:NT * NE].rearrange("p (t e) -> p t e", t=NT),
                                   r(BASE).unsqueeze(1).to_broadcast([P, NT, NE]), ALU.add))
            for k in range(TOPK):
                link(dve.tensor_tensor(tmpO, OH[:, k], Gx, ALU.mult))
                link(dve.tensor_reduce(small[:, 0:8], tmpO, AX_X, ALU.add))
                link(dve.tensor_copy(dest[:, k], small[:, 0:8]))
            dve.nop().then_inc(dest_ready, 1)
            U = small[:, 16:32]
            uf = U[:, 0:1]
            link(dve.tensor_copy(uf, slotid[:, 0, 0:1]))
            link(dve.tensor_scalar(r(T0), r(IU), uf, None, ALU.is_le))
            link(dve.tensor_reduce(U[:, 1:2], r(T0), AX_X, ALU.add))
            link(dve.tensor_scalar(r(T0), iot, U[:, 1:2], None, ALU.is_equal))
            for i, src in enumerate((CNT, US, BASE)):
                link(dve.tensor_tensor(r(T1), r(T0), r(src), ALU.mult))
                link(dve.tensor_reduce(U[:, 2 + i:3 + i], r(T1), AX_X, ALU.add))
            link(dve.tensor_tensor(U[:, 5:6], uf, U[:, 3:4], ALU.subtract))
            link(dve.tensor_scalar(U[:, 5:6], U[:, 5:6], float(WU), None, ALU.mult))
            link(dve.tensor_tensor(U[:, 6:7], U[:, 2:3], U[:, 5:6], ALU.subtract))
            link(dve.tensor_scalar(U[:, 6:7], U[:, 6:7], 0.0, float(STEP - 1), ALU.max, ALU.add))
            link(dve.tensor_copy(U[:, 7:8].bitcast(I32), U[:, 6:7]))
            link(dve.tensor_scalar(U[:, 8:9].bitcast(I32), U[:, 7:8].bitcast(I32), 5, None, ALU.logical_shift_right))
            link(dve.tensor_scalar(U[:, 10:11], U[:, 8:9].bitcast(I32), float(P // STEP), float(NCLS), ALU.max, ALU.min))
            link(dve.tensor_scalar(U[:, 11:12], U[:, 6:7], float(STEP), None, ALU.is_ge))
            link(dve.tensor_tensor(tabc[:, 0:1], U[:, 10:11], U[:, 11:12], ALU.mult))
            link(dve.tensor_scalar(tabc[:, 1:2], U[:, 1:2], float(NE - 1), None, ALU.min))
            link(dve.tensor_tensor(U[:, 9:10], U[:, 4:5], U[:, 5:6], ALU.add))
            link(dve.tensor_scalar(tabc[:, 2:3], U[:, 9:10], 1.0 / P, float(BLOCKS - 2), ALU.mult, ALU.min))
            link(dve.tensor_copy(tabc[:, 3:4], r(IU)[:, NE - 1:NE]))
            dve.nop().then_inc(tab_col, 1)
            dve.wait_ge(bias_turned, 1)
            link(dve.tensor_copy(bgT, ps[7][:, 0:KD * NE].rearrange("p (k e) -> p k e", k=KD)))
            link(dve.tensor_scalar(buT, ps[7][:, KD * NE:2 * KD * NE].rearrange("p (k e) -> p k e", k=KD), 1.0, None, ALU.add))
            dve.nop().then_inc(bias_ready, 1)
            dve.wait_ge(x1_ready, NT)
            dve.wait_ge(h2_ready, NT)
            link(dve.tensor_scalar(X1, X1, ALPHA, None, ALU.mult))
            for T in range(NT):
                for s in range(2):
                    q = slice(s * BANK, (s + 1) * BANK)
                    dve.wait_ge(bd_mm, 2 * T + s + 1)
                    if T:
                        dve.wait_ge(bd_used, 2 * T + s - 1)
                    link(dve.tensor_tensor(xres[:, s, 0:BANK], ps[2 + s][:, :], adarow[:, 3, q], ALU.mult))
                    dve.tensor_tensor(X1[:, T, q], X1[:, T, q], xres[:, s, 0:BANK], ALU.add).then_inc(bd_used, 1)
            dve.wait_ge(bd_used, 2 * NT)
            dve.wait_ge(dest_ready, 1)
            link(dve.memset(act_, 0.0))
            link(dve.memset(yb, 0.0))
            dve.wait_ge(d_rowslot, 16)
            link(dve.tensor_scalar(rowtok, rowslot, SEQ - 1, None, ALU.bitwise_and))
            dve.nop().then_inc(moe_clear, 1)
            dve.wait_ge(tab_ready, 16)
            for b in range(2):
                dve.nop().then_inc(y_dve[b], 1)
            with dve.Fori(0, MAXU) as u:
                cls = dve.value_load(tab[0:1, ds(u * 4, 1)], min_val=0, max_val=NCLS)
                with dve.If(cls > 0):
                    e = dve.value_load(tab[0:1, ds(u * 4 + 1, 1)], min_val=0, max_val=NE - 1)
                    dve.tensor_copy(bgc.unsqueeze(2), bgT[:, :, ds(e, 1)]).then_inc(bias_now, 1)
                    dve.tensor_copy(buc.unsqueeze(2), buT[:, :, ds(e, 1)]).then_inc(bias_now, 1)
                    for v in CLASSES:
                        with dve.If(cls == v):
                            n = STEP * v
                            dve.wait_ge(bias_now, 2 * u + 2)
                            for m in range(KD):
                                if m % 2 == 0 and m < 6:
                                    dve.wait_ge(gate_mm, 3 * u + m // 2 + 1)
                                elif m == 6:
                                    dve.wait_ge(w_used, PIECES * u + 4)
                                dve.tensor_scalar(gb[:, m, 0:n], ps[m // 2][:, (m % 2) * WU:(m % 2) * WU + n],
                                                  bgc[:, m:m + 1], LIMIT, ALU.add, ALU.min).then_inc(g_ready, 1)
                            for m in range(0, KD, 2):
                                dve.wait_ge(sg_ready, 4 * u + m // 2 + 1)
                                dve.tensor_tensor(gb[:, m:m + 2, 0:n], gb[:, m:m + 2, 0:n], sg[:, m:m + 2, 0:n],
                                                  ALU.mult).then_inc(gs_ready, 1)
                            dve.wait_ge(gs_ready, 4 * u + 4)
                            for m in range(KD + 1):
                                if m % 2 == 0 and m < 6:
                                    dve.wait_ge(up_mm, 3 * u + m // 2 + 1)
                                elif m == 6:
                                    dve.wait_ge(w_used, PIECES * u + 8)
                                if m < KD:
                                    dve.tensor_scalar(sg[:, m, 0:n], ps[4 + m // 2][:, (m % 2) * WU:(m % 2) * WU + n],
                                                      buc[:, m:m + 1], 1.0 - LIMIT, ALU.add, ALU.max).then_inc(t_ready, 1)
                                if m:
                                    dve.wait_ge(t_ready, 8 * u + m)
                                    dve.scalar_tensor_tensor(out=act_[:, m - 1, 0:n], in0=sg[:, m - 1, 0:n],
                                                             scalar=1.0 + LIMIT, in1=gb[:, m - 1, 0:n], op0=ALU.min,
                                                             op1=ALU.mult).then_inc(act_ready, 1)
                    dve.wait_ge(yb_free, u + 1)
                    dve.wait_ge(w_used, PIECES * u + PIECES)
                    dve.tensor_copy(yb[:, 0, BANK:D], ps[5][:, :]).then_inc(y_dve[0], 1)
                    with dve.If(cls > P // STEP):
                        dve.tensor_copy(yb[:, 1, BANK:D], ps[7][:, :]).then_inc(y_dve[1], 1)
                    with dve.If(cls <= P // STEP):
                        dve.nop().then_inc(y_dve[1], 1)
                    dve.nop()
            dve.wait_ge(d_ln2, 32)
            for T in range(NT):
                a = acc[:, T % 2]
                if T:
                    dve.wait_ge(xn_ready, T)
                dve.wait_ge(y0_scaled, T + 1)
                for k in range(1, TOPK):
                    mm = dve.scalar_tensor_tensor(out=a, in0=yrows[T % 2][:, k], scalar=topw[:, T, k:k + 1], in1=a,
                                                  op0=ALU.mult, op1=ALU.add)
                    link(mm)
                dve.nop().then_inc(yr_used, 1)
                link(dve.tensor_tensor(a, a, adarow[:, 3], ALU.mult))
                link(dve.tensor_tensor(a, a, X1[:, T], ALU.add))
                stats(a)
                link(dve.scalar_tensor_tensor(out=small[:, 50:51], in0=mv[:, 0:1], scalar=-1.0, in1=small[:, 49:50],
                                              op0=ALU.mult, op1=ALU.mult))
                dve.nop().then_inc(xn_in, 1)

        @block.gpsimd
        def _(pool):
            ch = Chain(pool, pch)
            link = ch.link
            link(pool.memset(ident[:, :], 0.0))
            pool.affine_select(out=ident[:, :], in_=ident[:, :], compare_op=ALU.not_equal, fill=1.0, base=0,
                               pattern=[[-1, P]], channel_multiplier=1).then_inc(const_ready, 1)
            pool.memset(lruw[:, :, :], 0.0).then_inc(const_ready, 1)
            link(pool.memset(ones[:, :], 1.0))
            link(pool.memset(eps_ln[:, :], LN_EPS))
            link(pool.memset(eps_rms[:, :], RMS_EPS))
            link(pool.affine_select(out=tri[:, :], in_=ones[:, :], compare_op=ALU.is_gt, fill=0.0, base=0,
                                    pattern=[[1, P]], channel_multiplier=-1))
            mf = fmask
            for d in range(2):
                sgn = 1 - 2 * d
                link(pool.affine_select(out=mf, in_=ones[:, :], compare_op=ALU.is_ge, fill=0.0, base=0,
                                        pattern=[[sgn, P]], channel_multiplier=-sgn))
                if d == 0:
                    link(pool.memset(mf[0:CH, CH:P], 0.0))
                else:
                    link(pool.memset(mf[CH:P, 0:CH], 0.0))
                link(pool.tensor_copy(masks[:, d, :], mf))
            pool.nop().then_inc(const_ready, 1)
            for i in range(2 * JL):
                pool.wait_ge(lru_sig, 6 * i + 6)
                pool.tensor_tensor(lC, lC, XL[:, i // 2], ALU.mult).then_inc(lru_ix, 1)
            for t in range(NT):
                pool.wait_ge(x1_ready, t + 1)
                if t >= 2:
                    pool.wait_ge(h2_stored[t % 2], 16 * (t // 2))
                    pool.wait_ge(h2_turned, 2 * (t - 1))
                link(pool.tensor_tensor(h2b[:, t % 2], X1[:, t], adarow[:, 2], ALU.mult))
                pool.tensor_tensor(h2b[:, t % 2], h2b[:, t % 2], adarow[:, 1], ALU.add).then_inc(h2_ready, 1)
            for b in range(2):
                pool.wait_ge(h2_stored[b], 8 * NT)
            pool.wait_ge(h2_turned, 2 * NT)
            pool.iota(slotid, pattern=[[SEQ, TOPK], [P, NT]], base=0, channel_multiplier=1).then_inc(iota_ready, 1)
            pool.iota(ioti2, pattern=[[1, NE]], base=0, channel_multiplier=0).then_inc(iota_ready, 1)
            link(pool.memset(rowslot, NOSLOT))
            pool.dma_start(rowslot_dram.rearrange("(p n) a -> p (n a)", p=P), rowslot).then_inc(rt_zeroed, 16)
            pool.wait_ge(rt_zeroed, 16)
            pool.wait_ge(dest_ready, 1)
            pool.wait_ge(iota_ready, 2)
            for k in range(TOPK):
                for T in range(NT):
                    pool.indirect_dma_start(out=rowslot_dram, out_offset=bass.IndirectOffsetOnAxis(ap=dest[:, k, T:T + 1], axis=0),
                                            in_=slotid[:, k, T:T + 1], in_offset=None).then_inc(rt_scattered, 16)

            def scatter(b):
                pool.indirect_dma_start(out=y_dram, out_offset=bass.IndirectOffsetOnAxis(ap=sidx[:, b:b + 1], axis=0),
                                        in_=yb[:, b], in_offset=None, bounds_check=TOPK * SEQ - 1,
                                        oob_is_err=False).then_inc(y_stored, 16)

            pool.wait_ge(tab_ready, 16)
            pool.wait_ge(moe_clear, 1)
            pool.nop().then_inc(yb_free, 1)
            with pool.Fori(0, MAXU) as u:
                cls = pool.value_load(tab[0:1, ds(u * 4, 1)], min_val=0, max_val=NCLS)
                with pool.If(cls > 0):
                    blk = pool.value_load(tab[0:1, ds(u * 4 + 2, 1)], min_val=0, max_val=BLOCKS - 2)
                    with pool.If(u > 0):
                        pool.wait_ge(xg_ready, 32 * u)
                        pool.wait_ge(mx_turned[0], u)
                        settle(pool)
                        pool.wait_ge(mx_turned[1], u)
                        settle(pool)
                    pool.tensor_copy(gidx.bitcast(I32), rowtok[:, ds(blk, 2)]).then_inc(gidx_ready, 1)
                    pool.wait_ge(gidx_ready, u + 1)
                    settle(pool)
                    for b in range(2):
                        pool.indirect_dma_start(out=xg[:, b], out_offset=None, in_=h2_dram,
                                                in_offset=bass.IndirectOffsetOnAxis(ap=gidx[:, b:b + 1], axis=0)).then_inc(xg_ready, 16)
                    with pool.If(u > 0):
                        pool.wait_ge(y_act[0], u + 1)
                        settle(pool)
                        pool.wait_ge(y_act[1], u + 1)
                        settle(pool)
                        pool.wait_ge(y_dve[0], u + 1)
                        settle(pool)
                        pool.wait_ge(y_dve[1], u + 1)
                        settle(pool)
                        for b in range(2):
                            scatter(b)
                        pool.wait_ge(y_stored, 32 * u)
                        settle(pool)
                        pool.nop().then_inc(yb_free, 1)
                    pool.tensor_copy(sidx.bitcast(I32), rowslot[:, ds(blk, 2)]).then_inc(sidx_ready, 1)
                    pool.wait_ge(sidx_ready, 2 * u + 1)
                    settle(pool)
                    with pool.If(cls <= NCLS // 2):
                        pool.memset(sidx.bitcast(I32)[:, 1:2], NOSLOT)
                    pool.nop()
                    pool.tensor_copy(sidx.bitcast(I32)[:, 0:1], sidx.bitcast(I32)[:, 0:1]).then_inc(sidx_ready, 1)
                    pool.wait_ge(sidx_ready, 2 * u + 2)
                    settle(pool)
            nunits = pool.value_load(tab[0:1, 3:4], min_val=1, max_val=MAXU)
            pool.wait_ge(y_act[0], nunits + 1)
            settle(pool)
            pool.wait_ge(y_act[1], nunits + 1)
            settle(pool)
            pool.wait_ge(y_dve[0], nunits + 1)
            settle(pool)
            pool.wait_ge(y_dve[1], nunits + 1)
            settle(pool)
            for b in range(2):
                scatter(b)
            pool.wait_ge(d_ln2, 32)
            for T in range(NT):
                f = fin[:, T % 2]
                pool.wait_ge(xn_ready, T + 1)
                link(pool.tensor_tensor(f, f, ln2r[:, 0], ALU.mult))
                pool.tensor_tensor(f, f, ln2r[:, 1], ALU.add).then_inc(fin_ready, 1)


_INS = ['x', 'c', 'ctx', 'c_ctx', 'w_ada', 'b_ada', 'w_in', 'conv_w', 'conv_b', 'lru_wa', 'lru_ba', 'lru_wx', 'lru_bx',
        'lru_lam', 'gla_wa', 'gla_ba', 'gla_norm_g', 'w_out', 'ln1_g', 'ln1_b', 'w_router', 'b_router', 'w_gate',
        'b_gate', 'w_up', 'b_up', 'w_down', 'b_down', 'ln2_g', 'ln2_b']


def kernel(**inputs):
    import numpy as _np
    import concourse.bacc as _bacc
    from concourse import mybir as _mybir
    from concourse.bass_utils import run_bass_kernel_spmd as _run

    nc = _bacc.Bacc("TRN2", target_bir_lowering=False, num_devices=1)
    arrays, args = {}, []
    for name in _INS:
        a = _np.ascontiguousarray(inputs[name])
        arrays[f"in_{name}_dram"] = a
        args.append(nc.dram_tensor(f"in_{name}_dram", a.shape, _mybir.dt.from_np(a.dtype), kind="ExternalInput").ap())
    args.append(nc.dram_tensor("out_dram", inputs["x"].shape, _mybir.dt.float32, kind="ExternalOutput").ap())
    layer(nc, *args)
    r = _run(nc, [arrays], core_ids=[0])
    return r.results[0]["out_dram"]
```
